# Optimizing a Trainium2 kernel written in Bass

```python
import jax, jax.numpy as jnp
from jax import lax
import numpy as np

D_MODEL = 1024
BATCH = 1
SEQ = 512
DEPTH = 1

CHUNK = 64
D_MIX = D_MODEL
HEAD_DIM = 64
D_CONV = D_MIX // 2
D_SPATIAL = D_MIX - D_CONV
N_CONV_GROUPS = D_CONV // HEAD_DIM
N_SP_HEADS = D_SPATIAL // HEAD_DIM
N_MIX_HEADS = N_CONV_GROUPS + N_SP_HEADS
CONV_WIDTH = 3
SP_BLOCK = 128
D_IN = 3 * D_CONV + 2 * D_SPATIAL
N_EXPERTS = 16
N_EXPERT_GROUPS = 4
EXPERTS_PER_GROUP = N_EXPERTS // N_EXPERT_GROUPS
TOP_K = 2
D_EXPERT = D_MODEL // 2
N_ADA = 6
EPS = 1e-6

kernel_name = "hybrid_conv_gmlp_grouped_moe_adaln"

def rms_norm(x, g):
    xf = x.astype(jnp.float32)
    y = xf * lax.rsqrt(jnp.mean(xf * xf, axis=-1, keepdims=True) + EPS)
    return (y * g.astype(jnp.float32)).astype(x.dtype)

def modulate(h, shift, scale):
    return h * (1 + scale[:, None, :]) + shift[:, None, :]

def short_gated_conv(b_gate, c_gate, h, conv_w, conv_b):
    z = c_gate * h
    seq = z.shape[1]
    zp = jnp.pad(z, ((0, 0), (CONV_WIDTH - 1, 0), (0, 0)))
    acc = conv_b
    for k in range(CONV_WIDTH):
        acc = acc + conv_w[k] * zp[:, k:k + seq]
    return b_gate * acc

def spatial_gating(u, v, g_v, w_s, b_s):
    bsz, seq, _ = v.shape
    v = rms_norm(v, g_v)
    vb = v.reshape(bsz, seq // SP_BLOCK, SP_BLOCK, N_SP_HEADS, HEAD_DIM)
    pos = jnp.arange(SP_BLOCK)
    mask = (pos[None, :] // CHUNK) <= (pos[:, None] // CHUNK)
    w = jnp.where(mask[None], w_s, 0)
    s = jnp.einsum('hij,bnjhd->bnihd', w, vb) + b_s.T[None, None, :, :, None]
    return u * s.reshape(bsz, seq, D_SPATIAL)

def grouped_router(h, router_w, router_b):
    logits = h.astype(jnp.float32) @ router_w.astype(jnp.float32)
    scores = jax.nn.sigmoid(logits)
    sel = scores + router_b.astype(jnp.float32)
    n_tok = sel.shape[0]
    grp = sel.reshape(n_tok, N_EXPERT_GROUPS, EXPERTS_PER_GROUP)
    grp_score = lax.top_k(grp, 2)[0].sum(-1)
    top_group = jnp.argmax(grp_score, axis=-1)
    expert_group = jnp.arange(N_EXPERTS) // EXPERTS_PER_GROUP
    in_group = expert_group[None, :] == top_group[:, None]
    masked = jnp.where(in_group, sel, -jnp.inf)
    _, idx = lax.top_k(masked, TOP_K)
    w = jnp.take_along_axis(scores, idx, axis=-1)
    w = w / jnp.sum(w, axis=-1, keepdims=True)
    return jnp.sum(jax.nn.one_hot(idx, N_EXPERTS, dtype=jnp.float32) * w[..., None], axis=1)

def moe(h, router_w, router_b, w_gate, w_up, w_down):
    bsz, seq, d = h.shape
    hf = h.reshape(bsz * seq, d)
    combine = grouped_router(hf, router_w, router_b).astype(h.dtype)
    out = jnp.zeros_like(hf)
    for e in range(N_EXPERTS):
        act = jax.nn.silu(hf @ w_gate[e]) * (hf @ w_up[e])
        out = out + combine[:, e:e + 1] * (act @ w_down[e])
    return out.reshape(bsz, seq, d)

def setup_inputs(seed: int = 0) -> dict:
    key = jax.random.key(seed)
    ks = jax.random.split(key, 20)
    f32 = jnp.float32
    nrm = lambda k, shape, s: jax.random.normal(k, shape, f32) * s
    return {
        "x": nrm(ks[0], (BATCH, SEQ, D_MODEL), 1.0),
        "c": nrm(ks[1], (BATCH, D_MODEL), 1.0),
        "w_ada": nrm(ks[2], (DEPTH, D_MODEL, N_ADA * D_MODEL), 0.2 * D_MODEL ** -0.5),
        "b_ada": nrm(ks[3], (DEPTH, N_ADA * D_MODEL), 0.02),
        "norm1_g": 1.0 + nrm(ks[4], (DEPTH, D_MODEL), 0.02),
        "norm2_g": 1.0 + nrm(ks[5], (DEPTH, D_MODEL), 0.02),
        "w_in": nrm(ks[6], (DEPTH, D_MODEL, D_IN), D_MODEL ** -0.5),
        "conv_w": nrm(ks[7], (DEPTH, CONV_WIDTH, D_CONV), CONV_WIDTH ** -0.5),
        "conv_b": nrm(ks[8], (DEPTH, D_CONV), 0.02),
        "sp_norm_g": 1.0 + nrm(ks[9], (DEPTH, D_SPATIAL), 0.02),
        "sp_w": nrm(ks[10], (DEPTH, N_SP_HEADS, SP_BLOCK, SP_BLOCK), SP_BLOCK ** -0.5),
        "sp_b": 1.0 + nrm(ks[11], (DEPTH, N_SP_HEADS, SP_BLOCK), 0.02),
        "mix_out_g": 1.0 + nrm(ks[12], (DEPTH, D_MIX), 0.02),
        "w_out": nrm(ks[13], (DEPTH, D_MIX, D_MODEL), D_MIX ** -0.5),
        "router_w": nrm(ks[14], (D_MODEL, N_EXPERTS), D_MODEL ** -0.5),
        "router_b": nrm(ks[15], (N_EXPERTS,), 0.01),
        "exp_w_gate": nrm(ks[16], (DEPTH, N_EXPERTS, D_MODEL, D_EXPERT), D_MODEL ** -0.5),
        "exp_w_up": nrm(ks[17], (DEPTH, N_EXPERTS, D_MODEL, D_EXPERT), D_MODEL ** -0.5),
        "exp_w_down": nrm(ks[18], (DEPTH, N_EXPERTS, D_EXPERT, D_MODEL), D_EXPERT ** -0.5),
        "final_g": 1.0 + nrm(ks[19], (D_MODEL,), 0.02),
    }

def reference(x, c, w_ada, b_ada, norm1_g, norm2_g, w_in, conv_w, conv_b, sp_norm_g,
              sp_w, sp_b, mix_out_g, w_out, router_w, router_b, exp_w_gate, exp_w_up,
              exp_w_down, final_g):
    bsz, seq, _ = x.shape
    c_act = jax.nn.silu(c)
    split_pts = [D_CONV, 2 * D_CONV, 3 * D_CONV, 3 * D_CONV + D_SPATIAL]
    for l in range(DEPTH):
        ada = c_act @ w_ada[l] + b_ada[l]
        sh1, sc1, g1, sh2, sc2, g2 = jnp.split(ada, N_ADA, axis=-1)

        h = modulate(rms_norm(x, norm1_g[l]), sh1, sc1)
        proj = h @ w_in[l]
        b_gate, c_gate, hc, u, v = jnp.split(proj, split_pts, axis=-1)
        y_conv = short_gated_conv(b_gate, c_gate, hc, conv_w[l], conv_b[l])
        y_sp = spatial_gating(jax.nn.gelu(u), jax.nn.gelu(v), sp_norm_g[l], sp_w[l], sp_b[l])
        y = jnp.concatenate([y_conv, y_sp], axis=-1).reshape(bsz, seq, N_MIX_HEADS, HEAD_DIM)
        y = rms_norm(y, mix_out_g[l].reshape(N_MIX_HEADS, HEAD_DIM)).reshape(bsz, seq, D_MIX)
        x = x + g1[:, None, :] * (y @ w_out[l])

        h2 = modulate(rms_norm(x, norm2_g[l]), sh2, sc2)
        x = x + g2[:, None, :] * moe(h2, router_w, router_b, exp_w_gate[l], exp_w_up[l], exp_w_down[l])
    return rms_norm(x, final_g)


_drawn_inputs = setup_inputs


def setup_inputs(seed=0):
    import zlib

    import numpy as np

    out = dict(_drawn_inputs(seed))
    spreads = {}
    factors = {'norm1_g': 8.0,
     'norm2_g': 7.048,
     'conv_b': 64.0,
     'sp_norm_g': 8.0,
     'sp_b': 8.0,
     'mix_out_g': 8.0,
     'router_b': 4.941,
     'final_g': 7.967}
    for name, (base, spread) in spreads.items():
        noise = np.random.default_rng([zlib.crc32(name.encode()), seed]).standard_normal(out[name].shape)
        drawn = base * np.exp(spread * noise) if base else spread * noise
        out[name] = __import__('jax').numpy.asarray(drawn.astype(out[name].dtype))
    for name, factor in factors.items():
        out[name] = (out[name] * factor).astype(out[name].dtype)
    return out
```

```python
from contextlib import ExitStack

import concourse.bass as bass
from concourse import mybir

ALU = mybir.AluOpType
ACT = mybir.ActivationFunctionType
F32 = mybir.dt.float32
F32R = mybir.dt.float32r
F16 = mybir.dt.float16
I32 = mybir.dt.int32
AX = mybir.AxisListType

P = 128
BANK = 512
EPS = 1e-6
BIG = 1e30


def trunk_kernel(nc, x, c, w_ada, b_ada, norm1_g, norm2_g, w_in, conv_w, conv_b, sp_norm_g, sp_w,
                 sp_b, mix_out_g, w_out, router_w, router_b, exp_w_gate, exp_w_up, exp_w_down,
                 final_g, out):
    _, SEQ, D = x.shape
    E = router_w.shape[1]
    F = exp_w_gate.shape[3]
    T = SEQ // P
    CAP_TILES = SEQ // P
    K = D // P
    KF = F // P
    DC = conv_b.shape[1]
    DS = sp_norm_g.shape[1]
    H = sp_w.shape[1]
    HD = DS // H
    CT = DC // P
    G = 4
    assert SEQ == BANK and F == BANK and DC == BANK and DS == BANK and K == 8 and T == 4 and E == 16

    UNIT = 2048
    RING = 12
    PIECE = UNIT // 2
    SLOTS = 4
    CHUNK_COLS = [4, 3, 1, 2, 0]
    ada_units = {0: 0, 1: 18, 2: 26}
    chunk_units = [8, 10, 12, 14, 16, 34, 36]
    W_OUT_HALF = [1, 0]
    FIRST_MOE_UNIT = 38
    FIRST_MOE_PIECE = 28
    STEP_UNITS, STEP_PIECES = 6, 12

    def on_pool(n):
        return n % 3 == 2

    def pool_count(n):
        return sum(on_pool(m) for m in range(n))

    def dve_count(n):
        return sum(not on_pool(m) for m in range(n))

    POOL_STEP, DVE_STEP = pool_count(12), dve_count(12)
    POOL_0, DVE_0 = FIRST_MOE_PIECE + pool_count(8), dve_count(8)

    BASE = -(-nc.sbuf_base // 32) * 32
    KB = 1024
    RING_AT = BASE
    SPLIT_AT = RING_AT + RING * UNIT * 4
    X_AT = SPLIT_AT + SLOTS * 2 * PIECE * 4
    HT_AT = X_AT + T * D * 4
    A_AT = HT_AT + 32 * KB
    B_AT, C_AT = A_AT + 8 * KB, A_AT + 16 * KB
    S_AT = A_AT + 24 * KB
    CONST_AT = S_AT + 6 * KB

    def at(name, offset, shape, dt):
        return nc.alloc_sbuf_tensor_at(name, shape, dt, offset=offset)

    ring = at("ring", RING_AT, [P, RING, UNIT], F32)
    w_hi = at("w_hi", SPLIT_AT, [P, SLOTS, PIECE], F32R)
    w_lo = at("w_lo", SPLIT_AT + SLOTS * PIECE * 4, [P, SLOTS, PIECE], F32R)
    xs = at("xs", X_AT, [P, T, D], F32)
    hT_hi = at("hT_hi", HT_AT, [P, K, SEQ], F32R)
    hT_lo = at("hT_lo", HT_AT + 16 * KB, [P, K, SEQ], F32R)
    v_tok = at("v_tok", A_AT, [P, T, DS], F32)
    w_s = at("w_s", B_AT, [P, H, P], F32)
    u_tok = at("u_tok", B_AT, [P, T, DS], F32)
    diag1 = at("diag1", A_AT, [P, T, P], F32)
    square1 = at("square1", A_AT + 4 * KB, [P, D], F32)
    vrows = at("vrows", C_AT, [P, P], F32)
    ada0 = at("ada0", C_AT + 512, [P, BANK], F32)
    colrows = at("colrows", C_AT + 4 * KB, [16, P], F32)
    y_conv = at("y_conv", A_AT, [P, CT, SEQ], F32)
    z = at("z", C_AT, [P, CT, SEQ], F32)
    y_sq = at("y_sq", C_AT, [P, CT, SEQ], F32)
    conv_std = at("conv_std", B_AT + 4 * KB, [P, SEQ], F32)
    conv_r = at("conv_r", B_AT + 6 * KB, [P, SEQ], F32)
    ones_row = at("ones_row", B_AT, [P, P], F32)
    colrows2 = at("colrows2", B_AT + 1 * KB, [16, P], F32)
    g2_b = at("g2_b", C_AT, [P, D], F32)
    g1_b = at("g1_b", C_AT + 4 * KB, [P, D], F32)
    scale2_b = at("scale2_b", A_AT, [P, D], F32)
    shift2_b = at("shift2_b", A_AT + 4 * KB, [P, D], F32)
    h2_tok = at("h2_tok", B_AT, [P, 2, D], F32)
    wsT = at("wsT", S_AT, [P, H, P], F32)
    spg_b = at("spg_b", S_AT + 4 * KB, [P, DS], F32)
    ada1 = at("ada1", S_AT, [P, BANK], F32)
    ada2 = at("ada2", S_AT + 2 * KB, [P, BANK], F32)
    n2_row = at("n2_row", S_AT + 4 * KB, [P, BANK], F32)
    diag2 = at("diag2", S_AT, [P, T, P], F32)
    comb = at("comb", S_AT + 2 * KB, [P, T * E], F32)
    h2T = at("h2T", HT_AT, [P, K, SEQ], F32)
    xT_hi = at("xT_hi", HT_AT + 16 * KB, [P, K, P], F32R)
    xT_lo = at("xT_lo", HT_AT + 20 * KB, [P, K, P], F32R)
    fT_hi = at("fT_hi", HT_AT + 24 * KB, [P, KF, P], F32R)
    fT_lo = at("fT_lo", HT_AT + 26 * KB, [P, KF, P], F32R)
    rw = at("rw", HT_AT + 28 * KB, [P, K, E], F32)
    lgT = at("lgT", C_AT + 6 * KB, [E, SEQ], F32)
    act = at("act", HT_AT, [P, 2, F], F32)
    x_rows = at("x_rows", A_AT, [P, 2, D], F32)
    y_rows = at("y_rows", B_AT, [P, 2, D], F32)
    onehot = at("onehot", HT_AT + 12 * KB, [P, 2, T, P], F16)
    routing = at("routing", HT_AT + 4 * KB, [P, 28, T * E], F32)
    late = [C_AT + 4 * KB]

    def keep_late(name, cols, dt, parts=P):
        t = at(name, late[0], [parts, cols], dt)
        late[0] += -(-cols * (2 if dt == F16 else 4) // 32) * 32
        return t

    rankm = keep_late("rankm", T * E, F32)
    w_tok = keep_late("w_tok", 2 * T, F32)
    row_of = keep_late("row_of", 2 * T, I32)
    tok_of = keep_late("tok_of", E, I32)
    tok_now = keep_late("tok_now", 2, I32)
    slot_iota = keep_late("slot_iota", P, F32)
    tok_id = keep_late("tok_id", T, F16)
    over = keep_late("over", 64, I32)
    low_tri = keep_late("low_tri", P, F16)
    ones16 = keep_late("ones16", P, F16)
    rb_b = keep_late("rb_b", E, F32)
    mask16 = keep_late("mask16", T * E, F16)
    assert late[0] <= C_AT + 6 * KB
    head_ones4 = at("head_ones4", A_AT + 2 * KB, [P, P], F32)
    ov_w = at("ov_w", RING_AT, [P, 3, K * F], F32)
    ov_h2 = at("ov_h2", RING_AT + 48 * KB, [P, T, D], F32)
    ov_x = at("ov_x", RING_AT + 64 * KB, [P, K, P], F32)
    ov_act = at("ov_act", RING_AT + 68 * KB, [P, F], F32)
    ov_f = at("ov_f", RING_AT + 70 * KB, [P, KF, P], F32)
    ov_y = at("ov_y", RING_AT + 72 * KB, [P, D], F32)
    ov_pick = at("ov_pick", RING_AT + 76 * KB, [P, T, P], F32)
    ov_spread = at("ov_spread", RING_AT + 78 * KB, [P, T, P], F32)
    ov_rank = at("ov_rank", RING_AT + 80 * KB, [P, T], F32)
    ov_comb = at("ov_comb", RING_AT + 80 * KB + 64, [P, T], F32)
    out_sb = at("out_sb", RING_AT, [P, T, D], F32)
    y_back = at("y_back", RING_AT + 16 * KB, [P, T, 2, D], F32)
    fin_b = at("fin_b", RING_AT + 48 * KB, [P, D], F32)
    o = [CONST_AT]

    def keep(name, cols):
        t = at(name, o[0], [P, cols], F32)
        o[0] += -(-cols * 4 // 32) * 32
        return t

    ident = keep("ident", P)
    expand = keep("expand", P)
    head_ones = keep("head_ones", 32)
    vcols = keep("vcols", 56)
    mod1 = keep("mod1", 16)
    mod2 = keep("mod2", 16)
    st = keep("st", 96)
    assert o[0] <= nc.sbuf_usable_end, (o[0], nc.sbuf_usable_end)

    C_COL, N1_COL, N2_COL, MIX_COL, CW_COL, CB_COL, SPB_COL, NV = 0, 8, 16, 24, 32, 44, 48, 56
    ss1, r1, ssv, rv = st[:, 0:4], st[:, 4:8], st[:, 8:12], st[:, 12:16]
    ssp, rsp = st[:, 16:48], st[:, 48:80]
    ss2, r2, epsc = st[:, 80:84], st[:, 84:88], st[:, 88:89]

    with ExitStack() as ctx:
        bank = ctx.enter_context(nc.psum_tensor("bank", [P, 8, BANK], F32))

        def sem(name):
            return ctx.enter_context(nc.semaphore(name))

        h2_dram = nc.dram_tensor("h2_dram", [SEQ, D], F32).ap()
        y_dram = nc.dram_tensor("y_dram", [E * P, D], F32).ap()

        landed = [sem(f"unit_landed{s}") for s in range(RING)]
        x_in = [sem(f"x_in{t}") for t in range(T)]
        vec_in, ws_in, spg_in, n2_in, rw_in, rb_in, fin_in = map(sem, (
            "vectors_in", "w_s_in", "sp_gain_in", "norm2_row_in", "router_w_in", "router_b_in", "final_gain_in"))
        ada_b_in = [sem(f"ada_bias_in{q}") for q in range(3)]
        hi_ready, lo_pool, lo_dve, piece_used, ada_used = map(sem, (
            "hi_ready", "lo_by_pool", "lo_by_dve", "piece_used", "ada_unit_used"))
        step, pool_step = sem("dve_step"), sem("pool_step")
        consts, s_eps, s_ho, s_hones, s_expT, s_expand, s_ones, s_late = map(sem, (
            "identity_ready", "eps_ready", "head_ones_set", "head_ones_ready", "expand_turned", "expand_ready",
            "ones_row_ready", "late_constants"))
        s_vT, s_vcols, s_silu_c, s_ws_masked, s_wsT, s_wsT_sb = map(sem, (
            "vectors_turned", "vectors_ready", "silu_c_ready", "w_s_masked", "w_s_turned", "w_s_ready"))
        s_sq1, s_std1, s_diag1, s_xT, s_ada_row, s_colrows, s_cols, s_mod1 = map(sem, (
            "x_squares", "x_rms", "diag1_ready", "x_turned", "ada0_row_ready", "colrows_in", "columns_turned", "mod1_ready"))
        s_modded, s_hT = sem("h_modulated"), sem("h_split")
        s_chunk = sem("chunk_bank_done")
        s_gelu, s_vsq, s_vstd, s_vn, s_c, s_mixed, s_gated = map(sem, (
            "gelu_done", "v_squares", "v_rms", "v_normed", "c_ready", "v_mixed", "sp_gated"))
        s_z, s_spsq, s_spred, s_spstd, s_spn = map(sem, ("ch_ready", "sp_squares", "sp_sums", "sp_rms", "sp_normed"))
        s_y, s_ysq, s_nsum, s_nstd, s_rc, s_exp = map(sem, (
            "conv_y_ready", "conv_squares", "conv_sums", "conv_rms", "conv_r_ready", "conv_r_spread"))
        s_spT, s_sphi, s_yT = map(sem, ("sp_turned", "sp_hi_ready", "y_split"))
        s_adaq, s_bc, s_bcev, s_col2, s_cols2, s_mod2 = map(sem, (
            "ada_rows_ready", "row_spread", "row_kept", "colrows2_in", "columns2_turned", "mod2_ready"))
        s_x1, s_sq2, s_std2, s_diag2, s_x2T, s_h2T, s_lgT, s_lgTs, s_lg, s_exp2 = map(sem, (
            "x1_ready", "x1_squares", "x1_rms", "diag2_ready", "x1_turned", "h2T_ready", "logits_done", "logits_kept",
            "logits_turned", "router_exp"))
        s_h2a, s_h2b = sem("h2_scaled"), sem("h2_shifted")
        s_h2st = [sem("h2_stored0"), sem("h2_stored1")]
        s_mask, s_rank, s_oh, s_idx, s_tok, s_route = map(sem, (
            "mask_ready", "rank_done", "onehot_ready", "tokens_found", "tok_of_ready", "routing_done"))
        gathered = [sem("tokens_gathered0"), sem("tokens_gathered1")]
        s_xrTh, s_xThi, s_xTlo, s_silu, s_act, s_fT, s_fThi, s_fTlo, s_yev = map(sem, (
            "tokens_turned", "xT_hi_ready", "xT_lo_ready", "silu_done", "act_ready", "act_turned", "fT_hi_ready",
            "fT_lo_ready", "outputs_kept"))
        ov_in, ov_h2_in, ov_pe, ov_dve, ov_silu, ov_over = map(sem, (
            "overflow_weights_in", "overflow_tokens_in", "overflow_pe", "overflow_dve", "overflow_silu", "overflow_over"))
        y_stored = [sem("outputs_stored0"), sem("outputs_stored1")]
        s_back = [sem(f"outputs_back{t}") for t in range(T)]
        s_t1, s_t2, s_sq3, s_t3, s_r3, s_t4, out_st = map(sem, (
            "x1_y1_added", "x2_ready", "x2_squares", "x2_rms", "x2_r_ready", "out_ready", "out_stored"))

        def rt(n):
            return routing[:, n, :]

        def bank_k(b):
            return bank[:, b, :].rearrange("p (k n) -> p k n", n=P)

        row_f, over_f = routing[:, 23, 0:2 * T], routing[:, 24, :]

        def wait_bank(eng, n, b):
            if b < 3:
                eng.wait_ge(s_chunk, 3 * n + b + 1)
            else:
                eng.wait_ge(piece_used, 4 * n + 4)

        w_in_v = w_in[0].rearrange("(k p) n -> p k n", p=P)
        w_out_v = w_out[0].rearrange("(k p) n -> p k n", p=P)
        y_rows_dram = y_dram.rearrange("(e r) d -> e r d", e=E)

        def rows_of(w, e):
            return w[0, e].rearrange("(k p) n -> p k n", p=P)

        def chunk_unit(p):
            return chunk_units[p // 4] + (p % 4) // 2

        def moe_piece(h, n):
            return FIRST_MOE_PIECE + 8 + STEP_PIECES * h + n

        def moe_unit(p):
            return FIRST_MOE_UNIT + (p - FIRST_MOE_PIECE) // 2

        def raw_of(p):
            u = chunk_unit(p) if p < FIRST_MOE_PIECE else moe_unit(p)
            return ring[:, u % RING, (p % 2) * PIECE:(p % 2 + 1) * PIECE]

        OV_TILES = CAP_TILES - 1
        OV_PE, OV_DVE = 6, 9 + 2 * T

        def overflow(eng, tile, skip, before=None, expert=None):
            eng.wait_ge(s_route, 1)
            any_over = eng.value_load(over[0:1, 0:1], min_val=0, max_val=SEQ)
            with eng.If(any_over > 0):
                if before:
                    before()
                with eng.Fori(0, E) as e:
                    more = eng.value_load(over[0:1, bass.ds(e + E, 1)], min_val=0, max_val=SEQ)
                    with eng.If(more > 0):
                        if expert:
                            expert(e)
                        if tile:
                            with eng.Fori(0, OV_TILES) as j:
                                tile(e, j, e * OV_TILES + j)
                    with eng.Else():
                        count, per_expert = skip
                        eng.wait_ge(count, e * per_expert)
                        eng.sem_inc(count, per_expert)

        block = ctx.enter_context(nc.Block())

        @block.sync
        def _(sp):
            def freed(u):
                if u in range(0, 8) or u in range(18, 34):
                    sp.wait_ge(ada_used, (u if u < 8 else u - 10) + 1)
                elif u < FIRST_MOE_UNIT:
                    first = next(n for n in range(7) if chunk_units[n] <= u < chunk_units[n] + 2)
                    sp.wait_ge(lo_pool, 4 * first + 2 * (u - chunk_units[first]) + 2)
                else:
                    n = 2 * (u - FIRST_MOE_UNIT) + 2
                    sp.wait_ge(lo_pool, FIRST_MOE_PIECE + pool_count(n))
                    sp.wait_ge(lo_dve, dve_count(n))

            def load(u, src, k):
                sp.dma_start(slot_view(u, k), src).then_inc(landed[u % RING], 16)

            def slot_view(u, k):
                return ring[:, u % RING, :].rearrange("p (k n) -> p k n", k=k)

            for u in range(FIRST_MOE_UNIT):
                if u >= RING:
                    freed(u - RING)
                q = next((q for q in range(3) if ada_units[q] <= u < ada_units[q] + 8), None)
                if q is not None:
                    k = u - ada_units[q]
                    sp.dma_start(ring[:, u % RING, :], w_ada[0, k * P:(k + 1) * P, q * UNIT:(q + 1) * UNIT])\
                        .then_inc(landed[u % RING], 16)
                else:
                    n = next(n for n in range(7) if chunk_units[n] <= u < chunk_units[n] + 2)
                    half = u - chunk_units[n]
                    if n < 5:
                        j = CHUNK_COLS[n]
                        load(u, w_in_v[:, 4 * half:4 * half + 4, j * BANK:(j + 1) * BANK], 4)
                    else:
                        half = W_OUT_HALF[half]
                        load(u, w_out_v[:, 4 * half:4 * half + 4, (n - 5) * BANK:(n - 4) * BANK], 4)

            def expert_unit(u, n, e):
                if n < 4:
                    w = exp_w_gate if n < 2 else exp_w_up
                    load(u, rows_of(w, e)[:, 4 * (n % 2):4 * (n % 2) + 4, :], 4)
                else:
                    load(u, rows_of(exp_w_down, e - 1)[:, 2 * (n - 4):2 * (n - 4) + 2, :], 2)

            for u in range(FIRST_MOE_UNIT, FIRST_MOE_UNIT + 16):
                freed(u - RING)
                s, n = (0, u - 38) if u < 42 else ((u - 36) // 6, u % 6)
                expert_unit(u, n, s)

            def keep_y(e, parity, count):
                sp.wait_ge(s_yev, count)
                sp.dma_start(y_rows_dram[e, 0:P, :], y_rows[:, parity, :]).then_inc(y_stored[parity], 16)

            def load_step(i, h, store=True):
                for n in range(STEP_UNITS):
                    sp.wait_ge(piece_used, i * (2 * STEP_PIECES) + (moe_piece(h, 2 * n + 1) + 1))
                    expert_unit(54 + 6 * h + n, n, i * 2 + (3 + h))
                    if n == 3 and store:
                        keep_y(i * 2 + (h - 1), (h + 1) % 2, i * 4 + 2 * h)

            load_step(0, 0, store=False)
            load_step(0, 1)
            with sp.Fori(1, 6) as i:
                load_step(i, 0)
                load_step(i, 1)
            load_step(6, 0)
            for n in range(2):
                sp.wait_ge(lo_pool, POOL_0 + 13 * POOL_STEP + pool_count(2 * n + 2))
                sp.wait_ge(lo_dve, DVE_0 + 13 * DVE_STEP + dve_count(2 * n + 2))
                load(132 + n, rows_of(exp_w_down, E - 1)[:, 2 * n:2 * n + 2, :], 2)
            for e in range(12, E):
                keep_y(e, e % 2, 2 * e + 2)
            def ov_tokens():
                sp.wait_ge(lo_pool, POOL_0 + 15 * POOL_STEP + pool_count(4))
                sp.wait_ge(lo_dve, DVE_0 + 15 * DVE_STEP + dve_count(4))
                sp.dma_start(ov_h2[:], h2_dram.rearrange("(t p) d -> p t d", p=P)).then_inc(ov_h2_in, 16)

            def ov_weights(e):
                sp.wait_ge(ov_pe, e * (OV_TILES * OV_PE))
                for n, w in enumerate((exp_w_gate, exp_w_up, exp_w_down)):
                    src = w[0, bass.ds(e, 1)].rearrange("a (k p) n -> p (a k) n", p=P)
                    sp.dma_start(ov_w[:, n, :].rearrange("p (k n) -> p k n", n=w.shape[3]), src).then_inc(ov_in, 16)

            overflow(sp, None, (ov_in, 48), ov_tokens, ov_weights)
            sp.wait_ge(ov_over, 1)
            sp.wait_ge(lo_pool, POOL_0 + 15 * POOL_STEP + pool_count(4))
            sp.wait_ge(lo_dve, DVE_0 + 15 * DVE_STEP + dve_count(4))
            sp.dma_start(fin_b[:], final_g.rearrange("(a d) -> a d", a=1).broadcast_to([P, D])).then_inc(fin_in, 16)
            for t in range(T):
                sp.wait_ge(s_t4, t + 1)
                sp.dma_start(out[0, t * P:(t + 1) * P, :], out_sb[:, t, :]).then_inc(out_st, 16)
            sp.wait_ge(out_st, 16 * T)

        @block.gpsimd
        def _(pool):
            nc.gpsimd.memset(ident[:], 0.0).then_inc(pool_step, 1)
            pool.wait_ge(pool_step, 1)
            nc.gpsimd.affine_select(out=ident[:], in_=ident[:], compare_op=ALU.not_equal, fill=1.0,
                                    base=0, pattern=[[-1, P]], channel_multiplier=1).then_inc(consts, 1)

            def low(p, ready):
                pool.wait_ge(hi_ready, ready)
                nc.gpsimd.tensor_tensor(w_lo[:, p % SLOTS, :], raw_of(p), w_hi[:, p % SLOTS, :].bitcast(F32),
                                        ALU.subtract).then_inc(lo_pool, 1)

            def gather(e, parity, count, before=None):
                nc.gpsimd.tensor_copy(tok_now[:, parity:parity + 1], tok_of[:, bass.ds(e, 1)]).then_inc(pool_step, 1)
                pool.wait_ge(pool_step, count + 2)
                if before:
                    before()
                pool.indirect_dma_start(x_rows[:, parity, :], None, h2_dram,
                                        bass.IndirectOffsetOnAxis(ap=tok_now[:, parity:parity + 1], axis=0))\
                    .then_inc(gathered[parity], 16)

            for p in range(FIRST_MOE_PIECE):
                low(p, p + 1)
            pool.wait_ge(s_x1, 2 * T)
            nc.gpsimd.iota(slot_iota[:], pattern=[[1, P]], base=0, channel_multiplier=0,
                           allow_small_or_imprecise_dtypes=True).then_inc(s_late, 1)
            nc.gpsimd.iota(tok_id[:], pattern=[[P, T]], base=0, channel_multiplier=1,
                           allow_small_or_imprecise_dtypes=True).then_inc(s_late, 1)
            nc.gpsimd.memset(ones16[:], 1.0).then_inc(s_late, 1)
            pool.wait_ge(s_late, 3)
            nc.gpsimd.affine_select(out=low_tri[:], in_=ones16[:], compare_op=ALU.is_gt, fill=0.0,
                                    base=0, pattern=[[1, P]], channel_multiplier=-1).then_inc(s_late, 1)
            for t in range(T):
                pool.wait_ge(s_h2a, t + 1)
                nc.gpsimd.tensor_tensor(h2_tok[:, t % 2, :], h2_tok[:, t % 2, :], shift2_b[:], ALU.add).then_inc(s_h2b, 1)
                pool.wait_ge(s_h2b, t + 1)
                pool.dma_start(h2_dram[t * P:(t + 1) * P, :], h2_tok[:, t % 2, :]).then_inc(s_h2st[t % 2], 16)
            low(FIRST_MOE_PIECE + 2, FIRST_MOE_PIECE + 3)
            for b in range(2):
                pool.wait_ge(s_h2st[b], 32)
            for e in range(2):
                pool.wait_ge(s_tok, e + 1)
                gather(e, e, e)
            low(FIRST_MOE_PIECE + 5, FIRST_MOE_PIECE + 6)
            pool.wait_ge(s_tok, E)
            pool.wait_ge(s_xrTh, 2)
            gather(2, 0, 2)

            def pool_step_of(i, h, fetch=True):
                def low_of(n):
                    low(moe_piece(h, n), i * 24 + (moe_piece(h, n) + 1))
                if fetch:
                    pool.wait_ge(s_xrTh, i * 4 + (2 * h + 4))
                    gather(i * 2 + (3 + h), (1 + h) % 2, i * 2 + (3 + h), lambda: low_of(2))
                else:
                    low_of(2)
                for n in range(3, STEP_PIECES):
                    if on_pool(n):
                        low_of(n)

            with pool.Fori(0, 6) as i:
                pool_step_of(i, 0)
                pool_step_of(i, 1)
            pool_step_of(6, 0)
            pool_step_of(6, 1, fetch=False)
            pool_step_of(7, 0, fetch=False)
            low(moe_piece(15, 2), moe_piece(15, 2) + 1)
            pool.wait_ge(ov_over, 1)
            pool.wait_ge(lo_dve, DVE_0 + 15 * DVE_STEP + dve_count(4))
            pool.wait_ge(s_route, 1)
            for b in range(2):
                pool.wait_ge(y_stored[b], 16 * (E // 2))
            for t in range(T):
                for c in range(2):
                    pool.indirect_dma_start(y_back[:, t, c, :], None, y_dram,
                                            bass.IndirectOffsetOnAxis(ap=row_of[:, 4 * c + t:4 * c + t + 1], axis=0))\
                        .then_inc(s_back[t], 16)

        @block.scalar
        def _(act_e):
            def vec(row, n, src):
                act_e.dma_start(vrows[row:row + n, :], src).then_inc(vec_in, 16)

            vec(C_COL, K, c.rearrange("b (k p) -> (b k) p", p=P))
            vec(N1_COL, K, norm1_g.rearrange("b (k p) -> (b k) p", p=P))
            vec(N2_COL, K, norm2_g.rearrange("b (k p) -> (b k) p", p=P))
            vec(MIX_COL, K, mix_out_g.rearrange("b (k p) -> (b k) p", p=P))
            vec(CW_COL, 3 * CT, conv_w.rearrange("b w (k p) -> (b w k) p", p=P))
            vec(CB_COL, CT, conv_b.rearrange("b (k p) -> (b k) p", p=P))
            vec(SPB_COL, H, sp_b[0])
            for t in range(T):
                act_e.dma_start(xs[:, t, :], x[0, t * P:(t + 1) * P, :]).then_inc(x_in[t], 16)
            act_e.dma_start(w_s[:], sp_w[0].rearrange("h i j -> i h j")).then_inc(ws_in, 16)
            act_e.dma_start(spg_b[:], sp_norm_g.broadcast_to([P, DS])).then_inc(spg_in, 16)

            def bias_rows(dst, q):
                for j in range(4):
                    col = q * UNIT + j * BANK
                    act_e.dma_start(dst[32 * j:32 * j + 1, :], b_ada[0:1, col:col + BANK]).then_inc(ada_b_in[q], 16)

            bias_rows(ada0, 0)
            act_e.wait_ge(s_vcols, 1)
            nc.scalar.activation(vcols[:, 0:K], vcols[:, 0:K], ACT.Silu).then_inc(s_silu_c, 1)
            act_e.wait_ge(s_eps, 1)
            for t in range(T):
                act_e.wait_ge(x_in[t], 16)
                nc.scalar.activation(square1[:], xs[:, t, :], ACT.Square, accum_out=ss1[:, t:t + 1]).then_inc(s_sq1, 1)
                act_e.wait_ge(s_sq1, t + 1)
            nc.scalar.activation(ss1, ss1, ACT.Sqrt, bias=epsc, scale=1.0 / D).then_inc(s_std1, 1)
            act_e.wait_ge(s_ada_row, 4)
            for j in range(4):
                act_e.dma_start(colrows[4 * j:4 * j + 4, :], ada0[32 * j:32 * j + 1, :]).then_inc(s_colrows, 16)

            def high(p, u, i=0):
                if p % 2 == 0:
                    act_e.wait_ge(landed[u % RING], i * 16 + 16 * (u // RING + 1))
                if not (isinstance(i, int) and p < SLOTS):
                    act_e.wait_ge(piece_used, i * 24 + (p - SLOTS + 1))
                nc.scalar.activation(w_hi[:, p % SLOTS, :], raw_of(p), ACT.Copy).then_inc(hi_ready, 1)

            def high1(p):
                high(p, chunk_unit(p) if p < FIRST_MOE_PIECE else moe_unit(p))

            act_e.wait_ge(s_mod1, 2)
            for k in range(K):
                act_e.wait_ge(s_xT, k + 1)
                nc.scalar.activation(bank[:, k, :], bank[:, k, :], ACT.Identity, bias=mod1[:, k:k + 1],
                                     scale=mod1[:, 8 + k:9 + k]).then_inc(s_modded, 1)
                if k % 2:
                    high1(k // 2)
            for p in range(4, 8):
                high1(p)
            for t in range(T):
                wait_bank(act_e, 0, t)
                nc.scalar.activation(v_tok[:, t, :], bank[:, t, :], ACT.Gelu_apprx_tanh).then_inc(s_gelu, 1)
            for p in range(8, 12):
                high1(p)
            for t in range(T):
                wait_bank(act_e, 1, t)
                nc.scalar.activation(u_tok[:, t, :], bank[:, 4 + t, :], ACT.Gelu_apprx_tanh).then_inc(s_gelu, 1)
            act_e.wait_ge(s_vsq, 4)
            nc.scalar.activation(ssv, ssv, ACT.Sqrt, bias=epsc, scale=1.0 / DS).then_inc(s_vstd, 1)
            for p in range(12, 16):
                high1(p)
            for t in range(CT):
                wait_bank(act_e, 2, t)
                nc.scalar.activation(z[:, t, :], bank[:, t, :], ACT.Copy).then_inc(s_c, 1)
            act_e.wait_ge(s_gated, H)
            for t in range(T):
                nc.scalar.activation(bank[:, 4 + t, :], u_tok[:, t, :], ACT.Square).then_inc(s_spsq, 1)
            act_e.wait_ge(s_spred, T)
            nc.scalar.activation(ssp, ssp, ACT.Sqrt, bias=epsc, scale=1.0 / HD).then_inc(s_spstd, 1)
            bias_rows(ada1, 1)
            bias_rows(ada2, 2)
            for j in range(2):
                act_e.dma_start(n2_row[32 * j:32 * j + 1, :], norm2_g[0:1, j * BANK:(j + 1) * BANK]).then_inc(n2_in, 16)
            for p in range(16, 20):
                high1(p)
            for t in range(CT):
                act_e.wait_ge(s_y, t + 1)
                nc.scalar.activation(y_sq[:, t, :], y_conv[:, t, :], ACT.Square).then_inc(s_ysq, 1)
            for m in range(4):
                act_e.wait_ge(s_spT, m + 1)
                nc.scalar.activation(hT_hi[:, 4 + m, :], bank[:, m, :], ACT.Copy,
                                     scale=vcols[:, MIX_COL + 4 + m:MIX_COL + 5 + m]).then_inc(s_sphi, 1)
            for p in range(20, 24):
                high1(p)
            act_e.wait_ge(s_nsum, 1)
            nc.scalar.activation(conv_std[:], bank[:, 6, :], ACT.Sqrt, bias=epsc, scale=1.0 / HD).then_inc(s_nstd, 1)
            act_e.wait_ge(s_adaq, 10)
            for j in range(2):
                act_e.dma_start(colrows2[4 * j:4 * j + 4, :], ada1[64 + 32 * j:65 + 32 * j, :]).then_inc(s_col2, 16)
                act_e.dma_start(colrows2[8 + 4 * j:12 + 4 * j, :], ada2[32 * j:32 * j + 1, :]).then_inc(s_col2, 16)
            for n, dst in enumerate((g1_b, scale2_b, g2_b, shift2_b)):
                for half in range(2):
                    act_e.wait_ge(s_bc, 2 * n + half + 1)
                    nc.scalar.activation(dst[:, half * BANK:(half + 1) * BANK], bank[:, (2 * n + half) % 4, :],
                                         ACT.Copy).then_inc(s_bcev, 1)
                if n == 1:
                    high1(24)
                    high1(25)
            high1(26)
            high1(27)
            act_e.wait_ge(piece_used, FIRST_MOE_PIECE)
            act_e.dma_start(rw[:], router_w.rearrange("(k p) e -> p k e", p=P)).then_inc(rw_in, 16)
            for t in range(T):
                act_e.wait_ge(s_x1, T + t + 1)
                nc.scalar.activation(bank[:, 6:8, :].rearrange("p a b -> p (a b)"), xs[:, t, :], ACT.Square,
                                     accum_out=ss2[:, t:t + 1]).then_inc(s_sq2, 1)
                act_e.wait_ge(s_sq2, t + 1)
                nc.scalar.activation(ss2[:, t:t + 1], ss2[:, t:t + 1], ACT.Sqrt, bias=epsc,
                                     scale=1.0 / D).then_inc(s_std2, 1)
            act_e.dma_start(rb_b[:], router_b.rearrange("(a e) -> a e", a=1).broadcast_to([P, E])).then_inc(rb_in, 16)
            for k in range(K):
                act_e.wait_ge(s_x2T, k + 1)
                nc.scalar.activation(h2T[:, k, :], bank[:, k, :], ACT.Identity, bias=mod2[:, k:k + 1],
                                     scale=mod2[:, 8 + k:9 + k]).then_inc(s_h2T, 1)
            for p in range(28, 31):
                high1(p)
            act_e.wait_ge(s_lg, 1)
            nc.scalar.activation(rt(0), bank[:, 1, 0:T * E], ACT.Exp, scale=-1.0).then_inc(s_exp2, 1)
            high1(31)

            def turned_high(count):
                for half in range(2):
                    act_e.wait_ge(s_xrTh, count + half)
                    nc.scalar.activation(xT_hi[:, 4 * half:4 * half + 4, :], bank_k(4 + half), ACT.Copy).then_inc(s_xThi, 1)

            def act_high(count):
                act_e.wait_ge(s_fT, count)
                nc.scalar.activation(fT_hi[:], bank_k(4), ACT.Copy).then_inc(s_fThi, 1)

            def silu(parity, count):
                act_e.wait_ge(piece_used, count)
                nc.scalar.activation(act[:, parity, :], bank[:, 2 * parity, :], ACT.Silu).then_inc(s_silu, 1)

            turned_high(1)
            for p in range(32, 36):
                high1(p)
            silu(0, FIRST_MOE_PIECE + 4)
            turned_high(3)
            for n in range(4):
                high1(moe_piece(0, n))

            def act_step_of(i, h, turn=True):
                def high_of(n):
                    p = moe_piece(h, n)
                    high(p, moe_unit(p), i)
                for n in range(4, 8):
                    high_of(n)
                act_high(i * 2 + (h + 1))
                silu((1 + h) % 2, i * 24 + (moe_piece(h, 0) + 4))
                for n in range(8, 12):
                    high_of(n)
                if turn:
                    turned_high(i * 4 + (2 * h + 5))
                for n in range(12, 16):
                    high_of(n)

            with act_e.Fori(0, 7) as i:
                act_step_of(i, 0)
                act_step_of(i, 1)
            act_step_of(7, 0, turn=False)
            act_high(E)

            def ov_act_tile(e, j, tile):
                act_e.wait_ge(ov_pe, tile * OV_PE + 2)
                nc.scalar.activation(ov_act[:], bank[:, 2, :], ACT.Silu).then_inc(ov_silu, 1)

            overflow(act_e, ov_act_tile, (ov_silu, OV_TILES))
            for t in range(T):
                act_e.wait_ge(s_t2, t + 1)
                nc.scalar.activation(out_sb[:, t, :], xs[:, t, :], ACT.Square, accum_out=ss1[:, t:t + 1]).then_inc(s_sq3, 1)
                act_e.wait_ge(s_sq3, t + 1)
                nc.scalar.activation(ss1[:, t:t + 1], ss1[:, t:t + 1], ACT.Sqrt, bias=epsc, scale=1.0 / D).then_inc(s_t3, 1)

        @block.vector
        def _(dve):
            v = nc.vector
            chain = [0]

            def link(ins):
                chain[0] += 1
                ins.then_inc(step, 1)
                dve.wait_ge(step, chain[0])

            v.memset(epsc, EPS).then_inc(s_eps, 1)
            link(v.memset(head_ones4[:], 0.0))
            for j in range(4):
                v.memset(head_ones4[0:64, 32 * j:32 * j + 1], 1.0).then_inc(s_ho, 1)
                v.memset(head_ones4[64:P, 32 * j + 1:32 * j + 2], 1.0).then_inc(s_ho, 1)
            dve.wait_ge(s_ho, 8)
            v.tensor_copy(head_ones[:], head_ones4[:, 0:32]).then_inc(s_hones, 1)
            dve.wait_ge(s_vT, 1)
            v.tensor_copy(vcols[:], bank[:, 6, 0:NV]).then_inc(s_vcols, 1)
            dve.wait_ge(s_expT, 1)
            v.tensor_copy(expand[:], bank[:, 3, 0:P]).then_inc(s_expand, 1)
            dve.wait_ge(ws_in, 16)
            v.memset(w_s[0:64, :, 64:P], 0.0).then_inc(s_ws_masked, 1)
            for a in range(2):
                dve.wait_ge(s_wsT, a + 1)
                v.tensor_copy(wsT[:, 4 * a:4 * a + 4, :], bank_k(4 + a)).then_inc(s_wsT_sb, 1)
            dve.wait_ge(s_std1, 1)
            link(v.reciprocal(r1, ss1))
            dve.wait_ge(consts, 1)
            for t in range(T):
                v.tensor_scalar(diag1[:, t, :], ident[:], r1[:, t:t + 1], None, ALU.mult).then_inc(s_diag1, 1)
            dve.wait_ge(ada_b_in[0], 64)
            dve.wait_ge(ada_used, 8)
            for j in range(4):
                r = slice(32 * j, 32 * j + 1)
                v.tensor_tensor(ada0[r, :], ada0[r, :], bank[r, 7, :], ALU.add).then_inc(s_ada_row, 1)
            dve.wait_ge(s_cols, 1)
            v.tensor_copy(mod1[:, 0:8], bank[:, 6, 256:264]).then_inc(s_mod1, 1)
            v.scalar_tensor_tensor(out=mod1[:, 8:16], in0=bank[:, 6, 264:272], scalar=1.0,
                                   in1=vcols[:, N1_COL:N1_COL + 8], op0=ALU.add, op1=ALU.mult).then_inc(s_mod1, 1)
            for k in range(K):
                dve.wait_ge(s_modded, k + 1)
                link(v.tensor_copy(hT_hi[:, k, :], bank[:, k, :]))
                v.tensor_tensor(hT_lo[:, k, :], bank[:, k, :], hT_hi[:, k, :].bitcast(F32), ALU.subtract).then_inc(s_hT, 1)
            for t in range(T):
                dve.wait_ge(s_gelu, t + 1)
                v.tensor_tensor_reduce(bank[:, t, :], v_tok[:, t, :], v_tok[:, t, :], 1.0, 0.0, ALU.mult, ALU.add,
                                       ssv[:, t:t + 1]).then_inc(s_vsq, 1)
            dve.wait_ge(s_vstd, 1)
            link(v.reciprocal(rv, ssv))
            dve.wait_ge(spg_in, 16)
            for t in range(T):
                v.scalar_tensor_tensor(out=v_tok[:, t, :], in0=v_tok[:, t, :], scalar=rv[:, t:t + 1], in1=spg_b[:],
                                       op0=ALU.mult, op1=ALU.mult).then_inc(s_vn, 1)
            dve.wait_ge(s_gelu, 2 * T)
            for h in range(H):
                dve.wait_ge(s_mixed, h // 2 + 1)
                u_h = u_tok[:, :, h * HD:(h + 1) * HD]
                s_h = bank[:, 4 + h // 2, (h % 2) * 256:(h % 2 + 1) * 256].rearrange("p (t d) -> p t d", t=T)
                v.scalar_tensor_tensor(out=u_h, in0=s_h, scalar=vcols[:, SPB_COL + h:SPB_COL + h + 1], in1=u_h,
                                       op0=ALU.add, op1=ALU.mult).then_inc(s_gated, 1)
            for t in range(T):
                dve.wait_ge(s_spsq, t + 1)
                v.tensor_reduce(ssp[:, t * H:(t + 1) * H], bank[:, 4 + t, :].rearrange("p (h d) -> p h d", h=H),
                                AX.X, ALU.add).then_inc(s_spred, 1)
            dve.wait_ge(s_spstd, 1)
            link(v.reciprocal(rsp, ssp))
            for t in range(T):
                y_h = u_tok[:, t, :].rearrange("p (h d) -> p h d", h=H)
                v.tensor_tensor(y_h, y_h, rsp[:, t * H:(t + 1) * H].rearrange("p (h o) -> p h o", o=1).broadcast_to([P, H, HD]),
                                ALU.mult).then_inc(s_spn, 1)
            for t in range(CT):
                dve.wait_ge(s_c, t + 1)
                wait_bank(dve, 3, t)
                v.tensor_tensor(z[:, t, :], z[:, t, :], bank[:, t, :], ALU.mult).then_inc(s_z, 1)
                dve.wait_ge(s_z, t + 1)
                link(v.tensor_scalar(y_conv[:, t, :], z[:, t, :], vcols[:, CW_COL + 8 + t:CW_COL + 9 + t],
                                     vcols[:, CB_COL + t:CB_COL + t + 1], ALU.mult, ALU.add))
                for lag in (1, 2):
                    cw = CW_COL + 4 * (2 - lag) + t
                    link(v.scalar_tensor_tensor(out=y_conv[:, t, lag:], in0=z[:, t, :SEQ - lag], scalar=vcols[:, cw:cw + 1],
                                                in1=y_conv[:, t, lag:], op0=ALU.mult, op1=ALU.add))
            for t in range(CT):
                wait_bank(dve, 4, t)
                v.tensor_tensor(y_conv[:, t, :], y_conv[:, t, :], bank[:, 4 + t, :], ALU.mult).then_inc(s_y, 1)
            for m in range(4):
                dve.wait_ge(s_sphi, m + 1)
                v.scalar_tensor_tensor(out=hT_lo[:, 4 + m, :], in0=bank[:, m, :],
                                       scalar=vcols[:, MIX_COL + 4 + m:MIX_COL + 5 + m],
                                       in1=hT_hi[:, 4 + m, :].bitcast(F32), op0=ALU.mult, op1=ALU.subtract).then_inc(s_yT, 1)
            v.memset(ones_row[:], 1.0).then_inc(s_ones, 1)
            dve.wait_ge(ada_b_in[1], 64)
            dve.wait_ge(ada_used, 16)
            for j in range(4):
                r = slice(32 * j, 32 * j + 1)
                v.tensor_tensor(ada1[r, :], ada1[r, :], bank[r, 4, :], ALU.add).then_inc(s_adaq, 1)
            dve.wait_ge(s_nstd, 1)
            v.reciprocal(conv_r[:], conv_std[:]).then_inc(s_rc, 1)
            dve.wait_ge(ada_b_in[2], 64)
            dve.wait_ge(n2_in, 32)
            dve.wait_ge(ada_used, 24)
            for j in range(4):
                r = slice(32 * j, 32 * j + 1)
                v.tensor_tensor(ada2[r, :], ada2[r, :], bank[r, 5, :], ALU.add).then_inc(s_adaq, 1)
            dve.wait_ge(s_adaq, 8)
            for j in range(2):
                r = slice(32 * j, 32 * j + 1)
                v.scalar_tensor_tensor(out=ada2[r, :], in0=ada2[r, :], scalar=1.0, in1=n2_row[r, :],
                                       op0=ALU.add, op1=ALU.mult).then_inc(s_adaq, 1)
            for t in range(CT):
                dve.wait_ge(s_exp, t + 1)
                link(v.scalar_tensor_tensor(out=y_conv[:, t, :], in0=y_conv[:, t, :],
                                            scalar=vcols[:, MIX_COL + t:MIX_COL + t + 1], in1=bank[:, t, :],
                                            op0=ALU.mult, op1=ALU.mult))
                link(v.tensor_copy(hT_hi[:, t, :], y_conv[:, t, :]))
                v.tensor_tensor(hT_lo[:, t, :], y_conv[:, t, :], hT_hi[:, t, :].bitcast(F32), ALU.subtract).then_inc(s_yT, 1)
            dve.wait_ge(s_cols2, 1)
            v.tensor_copy(mod2[:], bank[:, 0, 0:16]).then_inc(s_mod2, 1)
            for half in range(2):
                if half == 0:
                    dve.wait_ge(s_bcev, 2)
                cols = slice(half * BANK, (half + 1) * BANK)
                for t in range(T):
                    b = t + 4 * (1 - half)
                    wait_bank(dve, 5 + half, t)
                    link(v.tensor_tensor(bank[:, b, :], bank[:, b, :], g1_b[:, cols], ALU.mult))
                    v.tensor_tensor(xs[:, t, cols], xs[:, t, cols], bank[:, b, :], ALU.add).then_inc(s_x1, 1)
            dve.wait_ge(s_col2, 64)
            dve.wait_ge(s_bcev, 8)
            for t in range(T):
                dve.wait_ge(s_std2, t + 1)
                link(v.reciprocal(r2[:, t:t + 1], ss2[:, t:t + 1]))
                v.tensor_scalar(diag2[:, t, :], ident[:], r2[:, t:t + 1], None, ALU.mult).then_inc(s_diag2, 1)
            for t in range(T):
                if t >= 2:
                    dve.wait_ge(s_h2st[t % 2], 16)
                v.scalar_tensor_tensor(out=h2_tok[:, t % 2, :], in0=xs[:, t, :], scalar=r2[:, t:t + 1], in1=scale2_b[:],
                                       op0=ALU.mult, op1=ALU.mult).then_inc(s_h2a, 1)
            dve.wait_ge(s_lgT, 1)
            v.tensor_copy(lgT[:], bank[0:E, 0, :]).then_inc(s_lgTs, 1)

            def r4(n, m=E):
                return routing[:, n, 0:T * m].rearrange("p (t e) -> p t e", t=T)

            scores, sel, S1, S2, oh1, oh2, M = r4(1), r4(2), r4(3), r4(4), r4(5), r4(6), r4(7)
            eidx, gidx, rowbase = r4(20), r4(21, G), r4(22)
            dve.wait_ge(s_exp2, 1)
            link(v.tensor_scalar(rt(8), rt(0), 1.0, None, ALU.add))
            link(v.reciprocal(rt(1), rt(8)))
            dve.wait_ge(rb_in, 16)
            link(v.tensor_tensor(sel, scores, rb_b[:].rearrange("p (o e) -> p o e", o=1).broadcast_to([P, T, E]), ALU.add))
            dve.wait_ge(s_late, 4)
            link(v.tensor_scalar(eidx, slot_iota[:, 0:E].rearrange("p (o e) -> p o e", o=1).broadcast_to([P, T, E]), 1.0, None, ALU.mult))
            link(v.tensor_scalar(rowbase, eidx, float(P), None, ALU.mult))
            link(v.tensor_copy(gidx, eidx[:, :, 0:G]))
            pair = rt(2).rearrange("p (g a b) -> p g a b", a=2, b=2)

            def half_of(n):
                return routing[:, n, 0:2 * T * G].rearrange("p (g a) -> p g a", a=2)

            link(v.tensor_tensor(half_of(9), pair[:, :, :, 0], pair[:, :, :, 1], ALU.max))
            link(v.tensor_tensor(half_of(10), pair[:, :, :, 0], pair[:, :, :, 1], ALU.min))

            def g1(n):
                return routing[:, n, 0:T * G]

            link(v.tensor_tensor(g1(11), half_of(9)[:, :, 0], half_of(9)[:, :, 1], ALU.max))
            link(v.tensor_tensor(g1(12), half_of(9)[:, :, 0], half_of(9)[:, :, 1], ALU.min))
            link(v.tensor_tensor(g1(13), half_of(10)[:, :, 0], half_of(10)[:, :, 1], ALU.max))
            link(v.tensor_tensor(g1(12), g1(12), g1(13), ALU.max))
            link(v.tensor_tensor(g1(11), g1(11), g1(12), ALU.add))

            def first_highest(values, idx, width, tmp, one):
                m = routing[:, tmp, 0:T]
                mb = m.rearrange("p (t o) -> p t o", o=1).broadcast_to([P, T, width])
                cand = r4(tmp + 1, width)
                link(v.tensor_reduce(m, values, AX.X, ALU.max))
                link(v.tensor_tensor(cand, values, mb, ALU.is_equal))
                link(v.scalar_tensor_tensor(out=cand, in0=cand, scalar=-2.0 * E, in1=idx, op0=ALU.mult, op1=ALU.add))
                link(v.tensor_reduce(m, cand, AX.X, ALU.min))
                link(v.tensor_tensor(one, cand, mb, ALU.is_equal))

            in_group = r4(14, G)
            first_highest(r4(11, G), gidx, G, 15, in_group)
            link(v.tensor_scalar(r4(17, G), in_group, BIG, -BIG, ALU.mult, ALU.add))
            gm = routing[:, 14, 0:T * G].rearrange("p (g o) -> p g o", o=1).broadcast_to([P, T * G, 4])
            gp = routing[:, 17, 0:T * G].rearrange("p (g o) -> p g o", o=1).broadcast_to([P, T * G, 4])
            link(v.tensor_tensor(rt(3).rearrange("p (g o) -> p g o", o=4), rt(2).rearrange("p (g o) -> p g o", o=4), gm, ALU.mult))
            link(v.tensor_tensor(rt(3).rearrange("p (g o) -> p g o", o=4), rt(3).rearrange("p (g o) -> p g o", o=4), gp, ALU.add))
            first_highest(S1, eidx, E, 15, oh1)
            link(v.scalar_tensor_tensor(out=S2, in0=oh1, scalar=-3 * BIG, in1=S1, op0=ALU.mult, op1=ALU.add))
            first_highest(S2, eidx, E, 15, oh2)
            link(v.tensor_tensor(M, oh1, oh2, ALU.add))
            v.tensor_copy(mask16[:], rt(7)).then_inc(s_mask, 1)
            for n, one in enumerate((oh1, oh2)):
                link(v.tensor_tensor(r4(15), one, scores, ALU.mult))
                link(v.tensor_reduce(routing[:, 18, n * T:(n + 1) * T], r4(15), AX.X, ALU.add))
            link(v.tensor_tensor(routing[:, 19, 0:T], routing[:, 18, 0:T], routing[:, 18, T:2 * T], ALU.add))
            link(v.reciprocal(routing[:, 19, T:2 * T], routing[:, 19, 0:T]))
            for n in range(2):
                link(v.tensor_tensor(w_tok[:, n * T:(n + 1) * T], routing[:, 18, n * T:(n + 1) * T], routing[:, 19, T:2 * T], ALU.mult))
            dve.wait_ge(s_rank, 1)
            link(v.scalar_tensor_tensor(out=rt(15), in0=bank[:, 2, 0:T * E], scalar=1.0, in1=rt(7), op0=ALU.add, op1=ALU.mult))
            link(v.tensor_scalar(rankm[:], rt(15), -1.0, None, ALU.add))

            def onehots(e):
                if e >= 2:
                    dve.wait_ge(s_idx, e - 1)
                for t in range(T):
                    v.tensor_scalar(onehot[:, e % 2, t, :], slot_iota[:], rankm[:, t * E + e:t * E + e + 1], None,
                                    ALU.is_equal).then_inc(s_oh, 1)

            def tokens(e):
                dve.wait_ge(s_idx, e + 1)
                v.tensor_copy(tok_of[:, e:e + 1], bank[:, 3 + 4 * (e % 2), 0:1]).then_inc(s_tok, 1)

            def low(p, ready):
                dve.wait_ge(hi_ready, ready)
                v.tensor_tensor(w_lo[:, p % SLOTS, :], raw_of(p), w_hi[:, p % SLOTS, :].bitcast(F32),
                                ALU.subtract).then_inc(lo_dve, 1)

            def low_static(ns):
                for n in ns:
                    if not on_pool(n):
                        low(FIRST_MOE_PIECE + n, FIRST_MOE_PIECE + n + 1)

            onehots(0)
            onehots(1)
            tokens(0)
            tokens(1)
            low_static(range(0, 4))
            for e in range(2, E):
                onehots(e)
                tokens(e)
            for n, one in enumerate((oh1, oh2)):
                link(v.tensor_tensor(r4(15 + n), one, w_tok[:, n * T:(n + 1) * T].rearrange("p (t o) -> p t o", o=1)
                                     .broadcast_to([P, T, E]), ALU.mult))
            link(v.tensor_tensor(comb[:], rt(15), rt(16), ALU.add))
            link(v.tensor_scalar(rt(17), rankm[:], float(P), None, ALU.is_lt))
            link(v.tensor_tensor(rt(15), rankm[:], rt(22), ALU.add))
            link(v.tensor_tensor(rt(15), rt(15), rt(17), ALU.mult))
            for n, one in enumerate((oh1, oh2)):
                link(v.tensor_tensor(r4(16), one, r4(15), ALU.mult))
                link(v.tensor_reduce(row_f[:, n * T:(n + 1) * T], r4(16), AX.X, ALU.add))
                link(v.tensor_tensor(r4(16), one, r4(17), ALU.mult))
                link(v.tensor_reduce(routing[:, 18, n * T:(n + 1) * T], r4(16), AX.X, ALU.add))
                link(v.tensor_tensor(w_tok[:, n * T:(n + 1) * T], w_tok[:, n * T:(n + 1) * T],
                                     routing[:, 18, n * T:(n + 1) * T], ALU.mult))
            link(v.tensor_copy(row_of[:], row_f))
            link(v.tensor_copy(over_f[0:1, 16:32], bank[0:1, 2, T * E:T * E + E]))
            link(v.tensor_reduce(over_f[0:1, 0:1], over_f[0:1, 16:32], AX.X, ALU.max))
            link(v.tensor_scalar(over_f[0:1, 0:1], over_f[0:1, 0:1], -float(P), 0.0, ALU.add, ALU.max))
            link(v.memset(over_f[0:1, 1:16], 0.0))
            for j in (2, 3):
                link(v.tensor_scalar(over_f[0:1, 16 * j:16 * j + 16], over_f[0:1, 16:32], -float(P * j), 0.0, ALU.add, ALU.max))
            link(v.tensor_scalar(over_f[0:1, 16:32], over_f[0:1, 16:32], -float(P), 0.0, ALU.add, ALU.max))
            v.tensor_copy(over[0:1, :], over_f[0:1, 0:64]).then_inc(s_route, 1)

            def turned_low(count):
                for half in range(2):
                    dve.wait_ge(s_xThi, count + half)
                    v.tensor_tensor(xT_lo[:, 4 * half:4 * half + 4, :], bank_k(4 + half),
                                    xT_hi[:, 4 * half:4 * half + 4, :].bitcast(F32), ALU.subtract).then_inc(s_xTlo, 1)

            def act_low(count):
                dve.wait_ge(s_fThi, count)
                v.tensor_tensor(fT_lo[:], bank_k(4), fT_hi[:].bitcast(F32), ALU.subtract).then_inc(s_fTlo, 1)

            def gated_act(parity, count, used):
                dve.wait_ge(s_silu, count)
                dve.wait_ge(piece_used, used)
                v.tensor_tensor(act[:, parity, :], act[:, parity, :], bank[:, 2 * parity + 1, :], ALU.mult).then_inc(s_act, 1)

            def keep_outputs(parity, used, stored=None):
                if stored is not None:
                    dve.wait_ge(y_stored[parity], stored)
                dve.wait_ge(piece_used, used)
                for half in range(2):
                    cols = slice(half * BANK, (half + 1) * BANK)
                    v.tensor_tensor(y_rows[:, parity, cols], bank[:, 6 + half, :], g2_b[:, cols], ALU.mult).then_inc(s_yev, 1)

            turned_low(1)
            low_static(range(4, 8))
            gated_act(0, 1, FIRST_MOE_PIECE + 8)
            turned_low(3)
            for n in range(4):
                if not on_pool(n):
                    low(moe_piece(0, n), moe_piece(0, n) + 1)

            def dve_step_of(i, h, turn=True, keep=True, stored=True):
                def low_of(n):
                    m = n % STEP_PIECES
                    if not on_pool(m):
                        low(moe_piece(h, n), i * 24 + (moe_piece(h, n) + 1))
                if keep:
                    keep_outputs((1 + h) % 2, i * 24 + moe_piece(h, 0), (i * 16 + (16 * h - 16)) if stored else None)
                for n in range(4, 8):
                    low_of(n)
                act_low(i * 2 + (h + 1))
                for n in range(8, 11):
                    low_of(n)
                gated_act((1 + h) % 2, i * 2 + (h + 2), i * 24 + (moe_piece(h, 0) + 8))
                low_of(11)
                if turn:
                    turned_low(i * 4 + (2 * h + 5))
                for n in range(12, 16):
                    low_of(n)

            dve_step_of(0, 0, keep=False)
            dve_step_of(0, 1, stored=False)
            with dve.Fori(1, 7) as i:
                dve_step_of(i, 0)
                dve_step_of(i, 1)
            dve_step_of(7, 0, turn=False)
            keep_outputs(0, moe_piece(15, 0), 16 * 7)
            act_low(E)
            keep_outputs(1, moe_piece(15, 4), 16 * 7)
            def ov_expert(e):
                dve.wait_ge(ov_h2_in, 16)
                dve.wait_ge(ov_dve, e * (OV_TILES * OV_DVE) + e * 2)
                v.tensor_copy(ov_rank[:], rankm[:].rearrange("p (t e) -> p t e", e=E)[:, :, bass.ds(e, 1)]
                              .rearrange("p t o -> p (t o)")).then_inc(ov_dve, 1)
                v.tensor_copy(ov_comb[:], comb[:].rearrange("p (t e) -> p t e", e=E)[:, :, bass.ds(e, 1)]
                              .rearrange("p t o -> p (t o)")).then_inc(ov_dve, 1)

            def ov_dve_tile(e, j, tile):
                base = tile * OV_DVE + e * 2 + 2
                pe_base = tile * OV_PE
                dve.wait_ge(ov_dve, base)
                v.tensor_scalar(ov_rank[:], ov_rank[:], -float(P), None, ALU.add).then_inc(ov_dve, 1)
                dve.wait_ge(ov_dve, base + 1)
                for t in range(T):
                    v.tensor_scalar(ov_pick[:, t, :], slot_iota[:], ov_rank[:, t:t + 1], None, ALU.is_equal).then_inc(ov_dve, 1)
                dve.wait_ge(ov_pe, pe_base + 1)
                for half in range(2):
                    v.tensor_copy(ov_x[:, 4 * half:4 * half + 4, :], bank_k(half)).then_inc(ov_dve, 1)
                for t in range(T):
                    v.tensor_scalar(ov_pick[:, t, :], ov_pick[:, t, :], ov_comb[:, t:t + 1], None, ALU.mult).then_inc(ov_dve, 1)
                dve.wait_ge(ov_pe, pe_base + 2)
                dve.wait_ge(ov_silu, tile + 1)
                v.tensor_tensor(ov_act[:], ov_act[:], bank[:, 3, :], ALU.mult).then_inc(ov_dve, 1)
                dve.wait_ge(ov_pe, pe_base + 3)
                v.tensor_copy(ov_f[:], bank_k(4)).then_inc(ov_dve, 1)
                dve.wait_ge(ov_pe, pe_base + 4)
                v.tensor_copy(ov_spread[:], bank_k(5)).then_inc(ov_dve, 1)
                dve.wait_ge(ov_pe, pe_base + 5)
                for half in range(2):
                    cols = slice(half * BANK, (half + 1) * BANK)
                    v.tensor_tensor(ov_y[:, cols], bank[:, 6 + half, :], g2_b[:, cols], ALU.mult).then_inc(ov_dve, 1)
                dve.wait_ge(ov_pe, pe_base + 6)
                v.tensor_tensor(xs[:].rearrange("p t (h n) -> p (t h) n", h=2), xs[:].rearrange("p t (h n) -> p (t h) n", h=2),
                                bank[:], ALU.add).then_inc(ov_dve, 1)

            overflow(dve, ov_dve_tile, (ov_dve, OV_TILES * OV_DVE + 2), None, ov_expert)
            v.memset(over_f[0:1, 1:2], 0.0).then_inc(ov_over, 1)

            def finish(t):
                dve.wait_ge(s_t3, t + 1)
                nc.vector.reciprocal(r1[:, t:t + 1], ss1[:, t:t + 1]).then_inc(s_r3, 1)
                dve.wait_ge(s_r3, t + 1)
                if t == 0:
                    dve.wait_ge(fin_in, 16)
                nc.vector.scalar_tensor_tensor(out=out_sb[:, t, :], in0=xs[:, t, :], scalar=r1[:, t:t + 1], in1=fin_b[:],
                                               op0=ALU.mult, op1=ALU.mult).then_inc(s_t4, 1)

            for t in range(T):
                dve.wait_ge(s_back[t], 32)
                for c in range(2):
                    v.scalar_tensor_tensor(out=xs[:, t, :], in0=y_back[:, t, c, :], scalar=w_tok[:, c * T + t:c * T + t + 1],
                                           in1=xs[:, t, :], op0=ALU.mult, op1=ALU.add).then_inc(s_t1 if c == 0 else s_t2, 1)
                    if c == 0:
                        dve.wait_ge(s_t1, t + 1)
                if t:
                    finish(t - 1)
            finish(T - 1)

        @block.tensor
        def _(pe):
            mm = nc.tensor.matmul
            pe.wait_ge(consts, 1)
            pe.wait_ge(vec_in, 16 * 7)
            nc.tensor.transpose(bank[:, 6, 0:NV], vrows[0:NV, :], ident[0:NV, 0:NV]).then_inc(s_vT, 1)
            pe.wait_ge(s_hones, 1)
            nc.tensor.transpose(bank[:, 3, 0:P], head_ones4[:], ident[:]).then_inc(s_expT, 1)
            pe.wait_ge(s_ws_masked, 1)
            for h in range(H):
                m = nc.tensor.transpose(bank[:, 4 + h // 4, (h % 4) * P:(h % 4 + 1) * P], w_s[:, h, :], ident[:])
                if h % 4 == 3:
                    m.then_inc(s_wsT, 1)

            def ada(q, b):
                for k in range(K):
                    u = ada_units[q] + k
                    pe.wait_ge(landed[u % RING], 16 * (u // RING + 1))
                    for j in range(4):
                        m = mm(bank[32 * j:32 * j + 1, b, :], vcols[:, k:k + 1], ring[:, u % RING, j * BANK:(j + 1) * BANK],
                               start=(k == 0), stop=(k == K - 1))
                    m.then_inc(ada_used, 1)

            pe.wait_ge(s_silu_c, 1)
            ada(0, 7)

            def turn_x(k, diag):
                for t in range(T):
                    m = mm(bank[:, k, t * P:(t + 1) * P], xs[:, t, k * P:(k + 1) * P], diag[:, t, :], start=True, stop=True)
                return m

            pe.wait_ge(s_diag1, T)
            pe.wait_ge(s_expand, 1)
            for k in range(4):
                turn_x(k, diag1).then_inc(s_xT, 1)
            pe.wait_ge(s_wsT_sb, 2)
            for k in range(4, 6):
                turn_x(k, diag1).then_inc(s_xT, 1)
            pe.wait_ge(s_colrows, 64)
            nc.tensor.transpose(bank[:, 6, 256:272], colrows[:], ident[0:16, 0:16]).then_inc(s_cols, 1)
            pe.wait_ge(s_mod1, 2)
            turn_x(6, diag1).then_inc(s_xT, 1)
            pe.wait_ge(s_ada_row, 4)
            turn_x(7, diag1).then_inc(s_xT, 1)

            def three(out_ap, lhs, rhs, first, last):
                (a_hi, a_lo), (b_hi, b_lo) = lhs, rhs
                mm(out_ap, a_hi, b_hi, start=first, stop=False)
                mm(out_ap, a_lo, b_hi, start=False, stop=False)
                return mm(out_ap, a_hi, b_lo, start=False, stop=last)

            def weights(p, cols):
                v = [w[:, p % SLOTS, :].rearrange("p (k n) -> p k n", n=BANK) for w in (w_hi, w_lo)]
                return lambda kk: (v[0][:, kk, cols], v[1][:, kk, cols])

            def chunk(n, first_bank, by_token, k_order=range(8), between=None):
                for q in range(4):
                    p = 4 * n + q
                    if n == 0:
                        pe.wait_ge(s_hT, max(2 * q + 2, 4))
                    pe.wait_ge(lo_pool, p + 1)
                    for b in range(4):
                        tile = slice(b * P, (b + 1) * P)
                        for kk in range(2):
                            k = k_order[2 * q + kk]
                            first, last = (q == 0 and kk == 0), (q == 3 and kk == 1)
                            if by_token:
                                m = three(bank[:, first_bank + b, :], (hT_hi[:, k, tile], hT_lo[:, k, tile]),
                                          weights(p, slice(0, BANK))(kk), first, last)
                            else:
                                m = three(bank[:, first_bank + b, :], weights(p, tile)(kk),
                                          (hT_hi[:, k, :], hT_lo[:, k, :]), first, last)
                        if q == 3 and b < 3:
                            m.then_inc(s_chunk, 1)
                    m.then_inc(piece_used, 1)
                    if between:
                        between(q)

            chunk(0, 0, True)
            pe.wait_ge(s_hT, K)
            chunk(1, 4, True)
            pe.wait_ge(s_gelu, T)
            pe.wait_ge(s_vsq, T)
            chunk(2, 0, False)
            pe.wait_ge(s_gelu, 2 * T)
            pe.wait_ge(s_vn, T)
            for h in range(H):
                m = mm(bank[:, 4 + h // 2, (h % 2) * 256:(h % 2 + 1) * 256], wsT[:, h, :],
                       v_tok[:, :, h * HD:(h + 1) * HD], start=True, stop=True)
                if h % 2:
                    m.then_inc(s_mixed, 1)
            pe.wait_ge(s_c, CT)
            chunk(3, 0, False)
            pe.wait_ge(s_spred, T)
            chunk(4, 4, False)
            pe.wait_ge(s_spn, T)
            pe.wait_ge(s_z, CT)
            for m_ in range(4):
                for t in range(T):
                    m = nc.tensor.transpose(bank[:, m_, t * P:(t + 1) * P], u_tok[:, t, m_ * P:(m_ + 1) * P], ident[:])
                m.then_inc(s_spT, 1)
            pe.wait_ge(s_y, CT)
            ada(1, 4)
            pe.wait_ge(s_ysq, CT)
            for t in range(CT):
                m = mm(bank[32 * t:32 * t + 32, 6, :], head_ones[:], y_sq[:, t, :], start=True, stop=True)
            m.then_inc(s_nsum, 1)
            ada(2, 5)
            pe.wait_ge(s_rc, 1)
            pe.wait_ge(s_yT, 4)
            for t in range(CT):
                mm(bank[:, t, :], expand[32 * t:32 * t + 32, :], conv_r[32 * t:32 * t + 32, :], start=True, stop=True).then_inc(s_exp, 1)

            rows = ((ada1, 0), (ada2, 0), (ada2, 64), (ada1, 64))

            def spread(n):
                src, r = rows[n]
                for half in range(2):
                    q = slice(r + 32 * half, r + 32 * half + 1)
                    mm(bank[:, (2 * n + half) % 4, :], ones_row[q, :], src[q, :], start=True, stop=True).then_inc(s_bc, 1)

            def in_o0(q):
                if q == 1:
                    pe.wait_ge(s_yT, 8)
                    pe.wait_ge(s_ones, 1)
                    pe.wait_ge(s_adaq, 10)
                    spread(0)
                    spread(1)
                if q == 2:
                    pe.wait_ge(s_bcev, 4)
                    spread(2)
                    spread(3)
                if q == 3:
                    pe.wait_ge(s_col2, 64)
                    pe.wait_ge(s_bcev, 8)
                    nc.tensor.transpose(bank[:, 0, 0:16], colrows2[:], ident[0:16, 0:16]).then_inc(s_cols2, 1)

            pe.wait_ge(s_adaq, 8)
            pe.wait_ge(s_nstd, 1)
            chunk(5, 4, True, [4, 5, 6, 7, 0, 1, 2, 3], in_o0)
            pe.wait_ge(s_mod2, 1)
            chunk(6, 0, True, [4, 5, 6, 7, 0, 1, 2, 3])
            pe.wait_ge(s_x1, 2 * T)
            pe.wait_ge(s_sq2, T)
            pe.wait_ge(s_diag2, T)
            for k in range(K):
                turn_x(k, diag2).then_inc(s_x2T, 1)
            pe.wait_ge(rw_in, 16)
            for k in range(K):
                pe.wait_ge(s_h2T, k + 1)
                m = mm(bank[0:E, 0, :], rw[:, k, :], h2T[:, k, :], start=(k == 0), stop=(k == K - 1))
            m.then_inc(s_lgT, 1)
            pe.wait_ge(s_lgTs, 1)
            pe.wait_ge(s_h2T, 2)
            for t in range(T):
                m = nc.tensor.transpose(bank[:, 1, t * E:(t + 1) * E], lgT[:, t * P:(t + 1) * P], ident[0:E, 0:E])
            m.then_inc(s_lg, 1)
            pe.wait_ge(s_mask, 1)
            for t in range(T):
                for s in range(t + 1):
                    mm(bank[:, 2, t * E:(t + 1) * E], low_tri[:] if s == t else ones16[:], mask16[:, s * E:(s + 1) * E],
                       start=(s == 0), stop=(s == t))
            for s in range(T):
                m = mm(bank[:, 2, T * E:T * E + E], ones16[:], mask16[:, s * E:(s + 1) * E], start=(s == 0), stop=(s == T - 1))
            m.then_inc(s_rank, 1)
            for e in range(E):
                pe.wait_ge(s_oh, 4 * e + 4)
                if e >= 2:
                    pe.wait_ge(s_tok, e - 1)
                for t in range(T):
                    m = mm(bank[:, 3 + 4 * (e % 2), 0:1], onehot[:, e % 2, t, :], tok_id[:, t:t + 1], start=(t == 0), stop=(t == T - 1))
                m.then_inc(s_idx, 1)

            def turn_rows(parity, count):
                pe.wait_ge(gathered[parity], count)
                for k in range(K):
                    m = nc.tensor.transpose(bank[:, 4 + k // 4, (k % 4) * P:(k % 4 + 1) * P],
                                            x_rows[:, parity, k * P:(k + 1) * P], ident[:])
                    if k == 3:
                        m.then_inc(s_xrTh, 1)
                m.then_inc(s_xrTh, 1)

            def in_proj(h, i, ns, first_bank):
                for q, n in enumerate(ns):
                    p = moe_piece(h, n) if h >= 0 else FIRST_MOE_PIECE + n
                    if h >= 0:
                        if on_pool(n):
                            pe.wait_ge(lo_pool, i * (2 * POOL_STEP) + (POOL_0 + POOL_STEP * h + pool_count(n + 1)))
                        else:
                            pe.wait_ge(lo_dve, i * (2 * DVE_STEP) + (DVE_0 + DVE_STEP * h + dve_count(n + 1)))
                    elif on_pool(n):
                        pe.wait_ge(lo_pool, FIRST_MOE_PIECE + pool_count(n + 1))
                    else:
                        pe.wait_ge(lo_dve, dve_count(n + 1))
                    for kk in range(2):
                        k = 2 * q + kk
                        m = three(bank[:, first_bank, :], (xT_hi[:, k, :], xT_lo[:, k, :]),
                                  weights(p, slice(0, BANK))(kk), k == 0, k == K - 1)
                    m.then_inc(piece_used, 1)

            def turn_act(parity, count):
                pe.wait_ge(s_act, count)
                for k in range(KF):
                    m = nc.tensor.transpose(bank[:, 4, k * P:(k + 1) * P], act[:, parity, k * P:(k + 1) * P], ident[:])
                m.then_inc(s_fT, 1)

            def out_proj(ps, waits):
                for k, p in enumerate(ps):
                    waits(k)
                    w = weights(p, slice(0, BANK))
                    for half in range(2):
                        m = three(bank[:, 6 + half, :], (fT_hi[:, k, :], fT_lo[:, k, :]), w(half), k == 0, k == KF - 1)
                    m.then_inc(piece_used, 1)

            turn_rows(0, 16)
            pe.wait_ge(s_xTlo, 2)
            in_proj(-1, 0, range(0, 4), 0)
            in_proj(-1, 0, range(4, 8), 1)
            turn_rows(1, 16)

            def pe_step_of(i, h, turn=True):
                par = (1 + h) % 2
                pe.wait_ge(s_xTlo, i * 4 + (2 * h + 4))
                in_proj(h, i, range(0, 4), 2 * par)
                turn_act(h % 2, i * 2 + (h + 1))
                in_proj(h, i, range(4, 8), 2 * par + 1)
                if turn:
                    pe.wait_ge(s_fTlo, i * 2 + (h + 1))
                    turn_rows(h % 2, i * 16 + 32)
                else:
                    pe.wait_ge(s_fTlo, i * 2 + (h + 1))
                if not (isinstance(i, int) and i == 0 and h == 0):
                    pe.wait_ge(s_yev, i * 4 + 2 * h)

                def waits(k):
                    n = 8 + k
                    if on_pool(n):
                        pe.wait_ge(lo_pool, i * (2 * POOL_STEP) + (POOL_0 + POOL_STEP * h + pool_count(n + 1)))
                    else:
                        pe.wait_ge(lo_dve, i * (2 * DVE_STEP) + (DVE_0 + DVE_STEP * h + dve_count(n + 1)))
                out_proj([moe_piece(h, 8 + k) for k in range(4)], waits)

            pe_step_of(0, 0)
            pe_step_of(0, 1)
            with pe.Fori(1, 7) as i:
                pe_step_of(i, 0)
                pe_step_of(i, 1)
            pe_step_of(7, 0, turn=False)
            turn_act(1, E)
            pe.wait_ge(s_fTlo, E)
            pe.wait_ge(s_yev, 2 * (E - 1))

            def last_waits(k):
                if on_pool(k):
                    pe.wait_ge(lo_pool, POOL_0 + POOL_STEP * 15 + pool_count(k + 1))
                else:
                    pe.wait_ge(lo_dve, DVE_0 + DVE_STEP * 15 + dve_count(k + 1))
            out_proj([moe_piece(15, k) for k in range(4)], last_waits)
            pe.wait_ge(s_yev, 2 * E)

            def ov_pe_tile(e, j, tile):
                base = tile * OV_DVE + e * 2 + 2
                wg, wu = (ov_w[:, n, :].rearrange("p (k n) -> p k n", n=F) for n in range(2))
                wd = ov_w[:, 2, :].rearrange("p (k n) -> p k n", n=D)
                pe.wait_ge(ov_dve, base + 5)
                for k in range(K):
                    for t in range(T):
                        m = mm(bank[:, k // 4, (k % 4) * P:(k % 4 + 1) * P], ov_h2[:, t, k * P:(k + 1) * P],
                               ov_pick[:, t, :], start=(t == 0), stop=(t == T - 1))
                m.then_inc(ov_pe, 1)
                pe.wait_ge(ov_in, e * 48 + 48)
                pe.wait_ge(ov_dve, base + 7)
                for b, w in ((2, wg), (3, wu)):
                    for k in range(K):
                        m = mm(bank[:, b, :], ov_x[:, k, :], w[:, k, :], start=(k == 0), stop=(k == K - 1))
                m.then_inc(ov_pe, 1)
                pe.wait_ge(ov_dve, base + 12)
                for k in range(KF):
                    m = nc.tensor.transpose(bank[:, 4, k * P:(k + 1) * P], ov_act[:, k * P:(k + 1) * P], ident[:])
                m.then_inc(ov_pe, 1)
                for t in range(T):
                    m = nc.tensor.transpose(bank[:, 5, t * P:(t + 1) * P], ov_pick[:, t, :], ident[:])
                m.then_inc(ov_pe, 1)
                pe.wait_ge(ov_dve, base + 13)
                for half in range(2):
                    for k in range(KF):
                        m = mm(bank[:, 6 + half, :], ov_f[:, k, :], wd[:, k, half * BANK:(half + 1) * BANK],
                               start=(k == 0), stop=(k == KF - 1))
                m.then_inc(ov_pe, 1)
                pe.wait_ge(ov_dve, base + 16)
                for t in range(T):
                    for half in range(2):
                        m = mm(bank[:, 2 * t + half, :], ov_spread[:, t, :], ov_y[:, half * BANK:(half + 1) * BANK],
                               start=True, stop=True)
                m.then_inc(ov_pe, 1)

            overflow(pe, ov_pe_tile, (ov_pe, OV_TILES * OV_PE))


_INS = ['x', 'c', 'w_ada', 'b_ada', 'norm1_g', 'norm2_g', 'w_in', 'conv_w', 'conv_b', 'sp_norm_g', 'sp_w', 'sp_b',
        'mix_out_g', 'w_out', 'router_w', 'router_b', 'exp_w_gate', 'exp_w_up', 'exp_w_down', 'final_g']


def kernel(**inputs):
    import numpy as _np
    import concourse.bacc as _bacc
    from concourse.bass_utils import run_bass_kernel_spmd as _run

    nc = _bacc.Bacc("TRN2", target_bir_lowering=False, num_devices=1)
    arrays, args = {}, []
    for name in _INS:
        a = _np.ascontiguousarray(inputs[name])
        arrays[f"in_{name}"] = a
        args.append(nc.dram_tensor(f"in_{name}", a.shape, mybir.dt.from_np(a.dtype), kind="ExternalInput").ap())
    out = nc.dram_tensor("out", inputs["x"].shape, F32, kind="ExternalOutput").ap()
    trunk_kernel(nc, *args, out)
    r = _run(nc, [arrays], core_ids=[0])
    return r.results[0]["out"]
```

```python
from contextlib import ExitStack

import concourse.bass as bass
from concourse import mybir

ALU = mybir.AluOpType
ACT = mybir.ActivationFunctionType
F32 = mybir.dt.float32
F32R = mybir.dt.float32r
F16 = mybir.dt.float16
I32 = mybir.dt.int32
AX = mybir.AxisListType

P = 128
BANK = 512
EPS = 1e-6
BIG = 1e30


def trunk_kernel(nc, x, c, w_ada, b_ada, norm1_g, norm2_g, w_in, conv_w, conv_b, sp_norm_g, sp_w,
                 sp_b, mix_out_g, w_out, router_w, router_b, exp_w_gate, exp_w_up, exp_w_down,
                 final_g, out):
    _, SEQ, D = x.shape
    E = router_w.shape[1]
    F = exp_w_gate.shape[3]
    T = SEQ // P
    CAP_TILES = SEQ // P
    K = D // P
    KF = F // P
    DC = conv_b.shape[1]
    DS = sp_norm_g.shape[1]
    H = sp_w.shape[1]
    HD = DS // H
    CT = DC // P
    G = 4
    assert SEQ == BANK and F == BANK and DC == BANK and DS == BANK and K == 8 and T == 4 and E == 16

    UNIT = 2048
    RING = 12
    PIECE = UNIT // 2
    SLOTS = 4
    CHUNK_COLS = [4, 3, 1, 2, 0]
    ada_units = {0: 0, 1: 16, 2: 26}
    chunk_units = [8, 10, 12, 14, 24, 34, 36]
    W_OUT_HALF = [1, 0]
    FIRST_MOE_UNIT = 38
    FIRST_MOE_PIECE = 28
    STEP_UNITS, STEP_PIECES = 6, 12

    def on_pool(n):
        return n % 3 == 2

    def pool_count(n):
        return sum(on_pool(m) for m in range(n))

    def dve_count(n):
        return sum(not on_pool(m) for m in range(n))

    POOL_STEP, DVE_STEP = pool_count(12), dve_count(12)
    POOL_0, DVE_0 = FIRST_MOE_PIECE + pool_count(8), dve_count(8)

    BASE = -(-nc.sbuf_base // 32) * 32
    KB = 1024
    RING_AT = BASE
    SPLIT_AT = RING_AT + RING * UNIT * 4
    X_AT = SPLIT_AT + SLOTS * 2 * PIECE * 4
    HT_AT = X_AT + T * D * 4
    A_AT = HT_AT + 32 * KB
    B_AT, C_AT = A_AT + 8 * KB, A_AT + 16 * KB
    S_AT = A_AT + 24 * KB
    CONST_AT = S_AT + 6 * KB

    def at(name, offset, shape, dt):
        return nc.alloc_sbuf_tensor_at(name, shape, dt, offset=offset)

    ring = at("ring", RING_AT, [P, RING, UNIT], F32)
    w_hi = at("w_hi", SPLIT_AT, [P, SLOTS, PIECE], F32R)
    w_lo = at("w_lo", SPLIT_AT + SLOTS * PIECE * 4, [P, SLOTS, PIECE], F32R)
    xs = at("xs", X_AT, [P, T, D], F32)
    hT_hi = at("hT_hi", HT_AT, [P, K, SEQ], F32R)
    hT_lo = at("hT_lo", HT_AT + 16 * KB, [P, K, SEQ], F32R)
    v_tok = at("v_tok", A_AT, [P, T, DS], F32)
    w_s = at("w_s", B_AT, [P, H, P], F32)
    u_tok = at("u_tok", B_AT, [P, T, DS], F32)
    diag1 = at("diag1", A_AT, [P, T, P], F32)
    square1 = at("square1", A_AT + 4 * KB, [P, D], F32)
    vrows = at("vrows", C_AT, [P, P], F32)
    ada0 = at("ada0", C_AT + 512, [P, BANK], F32)
    y_conv = at("y_conv", A_AT, [P, CT, SEQ], F32)
    z = at("z", C_AT, [P, CT, SEQ], F32)
    y_sq = at("y_sq", C_AT, [P, CT, SEQ], F32)
    conv_std = at("conv_std", B_AT + 4 * KB, [P, SEQ], F32)
    conv_r = at("conv_r", B_AT + 6 * KB, [P, SEQ], F32)
    g2_b = at("g2_b", C_AT, [P, D], F32)
    g1_b = at("g1_b", C_AT + 4 * KB, [P, D], F32)
    scale2_b = at("scale2_b", A_AT, [P, D], F32)
    shift2_b = at("shift2_b", A_AT + 4 * KB, [P, D], F32)
    h2_tok = at("h2_tok", B_AT, [P, 2, D], F32)
    wsT = at("wsT", S_AT, [P, H, P], F32)
    spg_b = at("spg_b", S_AT + 4 * KB, [P, DS], F32)
    ada1 = at("ada1", S_AT, [P, BANK], F32)
    ada2 = at("ada2", S_AT + 2 * KB, [P, BANK], F32)
    n2_row = at("n2_row", S_AT + 4 * KB, [P, BANK], F32)
    diag2 = at("diag2", S_AT, [P, T, P], F32)
    comb = at("comb", S_AT + 2 * KB, [P, T * E], F32)
    h2T = at("h2T", HT_AT, [P, K, SEQ], F32)
    xT_hi = at("xT_hi", HT_AT + 16 * KB, [P, K, P], F32R)
    xT_lo = at("xT_lo", HT_AT + 20 * KB, [P, K, P], F32R)
    fT_hi = at("fT_hi", HT_AT + 24 * KB, [P, KF, P], F32R)
    fT_lo = at("fT_lo", HT_AT + 26 * KB, [P, KF, P], F32R)
    rw = at("rw", S_AT + 4 * KB, [P, K, 32], F32)
    fold = at("fold", S_AT + 5 * KB, [P, 32], F32)
    lgT = at("lgT", C_AT + 6 * KB, [P, SEQ], F32)
    act = at("act", HT_AT, [P, 2, F], F32)
    x_rows = at("x_rows", A_AT, [P, 2, D], F32)
    y_rows = at("y_rows", B_AT, [P, 2, D], F32)
    numbers = at("numbers", HT_AT + 28 * KB, [P, T, E], F32)
    onehot = at("onehot", HT_AT + 12 * KB, [P, 2, T, P], F16)
    tok_val = at("tok_val", HT_AT + 11 * KB, [P, 2, T * E], F16)
    routing = at("routing", HT_AT + 4 * KB, [P, 28, T * E], F32)
    late = [C_AT + 4 * KB]

    def keep_late(name, cols, dt, parts=P):
        t = at(name, late[0], [parts, cols], dt)
        late[0] += -(-cols * (2 if dt == F16 else 4) // 32) * 32
        return t

    rankm = keep_late("rankm", T * E, F32)
    w_tok = keep_late("w_tok", 2 * T, F32)
    row_of = keep_late("row_of", 2 * T, I32)
    tok_of = keep_late("tok_of", E, I32)
    tok_now = keep_late("tok_now", 2, I32)
    slot_iota = keep_late("slot_iota", P, F32)
    tok_id = keep_late("tok_id", T, F16)
    over = keep_late("over", 64, I32)
    low_tri = keep_late("low_tri", P, F16)
    ones16 = keep_late("ones16", P, F16)
    rb_b = keep_late("rb_b", E, F32)
    mask16 = keep_late("mask16", T * E, F16)
    assert late[0] <= C_AT + 6 * KB
    head_ones4 = at("head_ones4", A_AT + 2 * KB, [P, P], F32)
    fin_b = at("fin_b", RING_AT + 8 * KB, [P, D], F32)
    y_back = at("y_back", RING_AT + 16 * KB, [P, T, 2, D], F32)
    out_sb = at("out_sb", RING_AT + 48 * KB, [P, T, D], F32)
    ov_rank = at("ov_rank", RING_AT, [P, T], F32)
    ov_comb = at("ov_comb", RING_AT + 64, [P, T], F32)
    ov_w = at("ov_w", RING_AT + 48 * KB, [P, 3, K * F], F32)
    ov_h2 = at("ov_h2", RING_AT + 96 * KB, [P, T, D], F32)
    ov_x = at("ov_x", RING_AT + 112 * KB, [P, K, P], F32)
    ov_act = at("ov_act", RING_AT + 116 * KB, [P, F], F32)
    ov_f = at("ov_f", RING_AT + 118 * KB, [P, KF, P], F32)
    ov_y = at("ov_y", RING_AT + 120 * KB, [P, D], F32)
    ov_pick = at("ov_pick", RING_AT + 124 * KB, [P, T, P], F32)
    ov_spread = at("ov_spread", RING_AT + 126 * KB, [P, T, P], F32)
    assert RING_AT + 128 * KB <= X_AT
    last_pick = at("last_pick", HT_AT + 12 * KB, [P, T, P], F32)
    last_spread = at("last_spread", HT_AT + 14 * KB, [P, T, P], F32)
    diag_w = at("diag_w", HT_AT + 12 * KB, [P, T, P], F32)
    o = [CONST_AT]

    def keep(name, cols):
        t = at(name, o[0], [P, cols], F32)
        o[0] += -(-cols * 4 // 32) * 32
        return t

    ident = keep("ident", P)
    expand = keep("expand", P)
    head_ones = keep("head_ones", 32)
    vcols = keep("vcols", 72)
    mod1 = mod2 = keep("mod", 16)
    st = keep("st", 96)
    assert o[0] <= nc.sbuf_usable_end, (o[0], nc.sbuf_usable_end)

    C_COL, N1_COL, N2_COL, MIX_COL, CW_COL, CB_COL, SPB_COL, ADA_COL, NV = 0, 8, 16, 24, 32, 44, 48, 56, 72
    ss1, r1, ssv, rv = st[:, 0:4], st[:, 4:8], st[:, 8:12], st[:, 12:16]
    ssp, rsp = st[:, 16:48], st[:, 48:80]
    ss2, r2, epsc = st[:, 80:84], st[:, 84:88], st[:, 88:89]

    with ExitStack() as ctx:
        bank = ctx.enter_context(nc.psum_tensor("bank", [P, 8, BANK], F32))

        def sem(name):
            return ctx.enter_context(nc.semaphore(name))

        h2_dram = nc.dram_tensor("h2_dram", [SEQ, D], F32).ap()
        y_dram = nc.dram_tensor("y_dram", [(E - 1) * P, D], F32).ap()
        rows_dram = nc.dram_tensor("rows_dram", [2, 4, BANK], F32).ap()

        K2_ORDER = (4, 5, 6, 7, 0, 1, 2, 3)

        landed = [sem(f"unit_landed{s}") for s in range(RING)]
        x_in = [sem(f"x_in{t}") for t in range(T)]
        vec_in, ws_in, spg_in, n2_in, rw_in, rb_in, fin_in = map(sem, (
            "vectors_in", "w_s_in", "sp_gain_in", "norm2_row_in", "router_w_in", "router_b_in", "final_gain_in"))
        ada_b_in = [sem(f"ada_bias_in{q}") for q in range(3)]
        hi_ready, lo_pool, lo_dve, piece_used, ada_used = map(sem, (
            "hi_ready", "lo_by_pool", "lo_by_dve", "piece_used", "ada_unit_used"))
        step, pool_step = sem("dve_step"), sem("pool_step")
        consts, s_eps, s_ho, s_hones, s_expT, s_expand, s_late = map(sem, (
            "identity_ready", "eps_ready", "head_ones_set", "head_ones_ready", "expand_turned", "expand_ready",
            "late_constants"))
        s_vT, s_vcols, s_silu_c, s_ws_masked, s_wsT, s_wsT_sb = map(sem, (
            "vectors_turned", "vectors_ready", "silu_c_ready", "w_s_masked", "w_s_turned", "w_s_ready"))
        s_sq1, s_std1, s_diag1, s_xT, s_ada_row, s_cols, s_mod1 = map(sem, (
            "x_squares", "x_rms", "diag1_ready", "x_turned", "ada0_row_ready", "columns_turned", "mod1_ready"))
        s_zeroed, s_fold, s_tokval = map(sem, ("ada_zeroed", "router_constants", "token_values_ready"))
        s_counts, s_h2T_dve, s_g1_in, s_rows_in, s_rows_out = map(sem, (
            "expert_counts_kept", "h2T_ready_dve", "gate1_in", "rows_in", "rows_out"))
        s_modded, s_hThi, s_hT = sem("h_modulated"), sem("h_hi_by_scalar"), sem("h_split")
        s_chunk = sem("chunk_bank_done")
        s_gelu, s_vsq, s_vstd, s_vn, s_c, s_mixed, s_gated = map(sem, (
            "gelu_done", "v_squares", "v_rms", "v_normed", "c_ready", "v_mixed", "sp_gated"))
        s_z, s_spsq, s_spred, s_spstd, s_spn = map(sem, ("ch_ready", "sp_squares", "sp_sums", "sp_rms", "sp_normed"))
        s_y, s_ysq, s_nsum, s_nstd, s_rc, s_exp = map(sem, (
            "conv_y_ready", "conv_squares", "conv_sums", "conv_rms", "conv_r_ready", "conv_r_spread"))
        s_spT, s_sphi, s_yT = map(sem, ("sp_turned", "sp_hi_ready", "y_split"))
        s_adaq, s_cols2, s_mod2 = map(sem, (
            "ada_rows_ready", "columns2_turned", "mod2_ready"))
        s_x1, s_sq2, s_std2, s_diag2, s_x2T, s_h2T, s_lgT, s_lgTs, s_lg, s_exp2 = map(sem, (
            "x1_ready", "x1_squares", "x1_rms", "diag2_ready", "x1_turned", "h2T_ready", "logits_done", "logits_kept",
            "logits_turned", "router_exp"))
        s_h2a, s_h2b = sem("h2_scaled"), sem("h2_shifted")
        s_h2st = [sem("h2_stored0"), sem("h2_stored1")]
        s_mask, s_rank, s_oh, s_idx, s_tok, s_route = map(sem, (
            "mask_ready", "rank_done", "onehot_ready", "tokens_found", "tok_of_ready", "routing_done"))
        gathered = [sem("tokens_gathered0"), sem("tokens_gathered1")]
        s_xrTh, s_xThi, s_xTlo, s_silu, s_act, s_fT, s_fThi, s_fTlo, s_yev = map(sem, (
            "tokens_turned", "xT_hi_ready", "xT_lo_ready", "silu_done", "act_ready", "act_turned", "fT_hi_ready",
            "fT_lo_ready", "outputs_kept"))
        ov_in, ov_h2_in, ov_pe, ov_dve, ov_silu = map(sem, (
            "overflow_weights_in", "overflow_tokens_in", "overflow_pe", "overflow_dve", "overflow_silu"))
        y_stored = [sem("outputs_stored0"), sem("outputs_stored1")]
        s_back = [sem(f"outputs_back{t}") for t in range(T)]
        s_pick, s_pickT, s_spread = map(sem, ("last_pick_ready", "last_pick_turned", "last_spread_ready"))
        s_diag_w, s_last = sem("diag_w_ready"), sem("outputs_spread")
        s_t1, s_t2, s_sq3, s_t3, s_r3, s_t4, out_st = map(sem, (
            "y2_added", "x2_ready", "x2_squares", "x2_rms", "x2_r_ready", "out_ready", "out_stored"))

        def rt(n):
            return routing[:, n, :]

        def bank_k(b):
            return bank[:, b, :].rearrange("p (k n) -> p k n", n=P)

        row_f, over_f, place_f = routing[:, 23, 0:2 * T], routing[:, 24, :], routing[:, 25, 0:2 * T]

        def row_of_dram(n, r):
            return rows_dram[n:n + 1, r:r + 2, :].rearrange("a r n -> a (r n)").broadcast_to([P, D])

        def turned_rows(b):
            return bank[:, b, :].rearrange("p (j r z) -> p r j z", r=4, z=32)[:, :, :, 0]

        def wait_bank(eng, n, b):
            if b < 3:
                eng.wait_ge(s_chunk, 3 * n + b + 1)
            else:
                eng.wait_ge(piece_used, 4 * n + 4)

        w_in_v = w_in[0].rearrange("(k p) n -> p k n", p=P)
        w_out_v = w_out[0].rearrange("(k p) n -> p k n", p=P)
        y_rows_dram = y_dram.rearrange("(e r) d -> e r d", r=P)

        def rows_of(w, e):
            return w[0, e].rearrange("(k p) n -> p k n", p=P)

        def ada_third(u):
            return next((q for q in range(3) if ada_units[q] <= u < ada_units[q] + K), None)

        def chunk_unit(p):
            return chunk_units[p // 4] + (p % 4) // 2

        def moe_piece(h, n):
            return FIRST_MOE_PIECE + 8 + STEP_PIECES * h + n

        def moe_unit(p):
            return FIRST_MOE_UNIT + (p - FIRST_MOE_PIECE) // 2

        def raw_of(p):
            u = chunk_unit(p) if p < FIRST_MOE_PIECE else moe_unit(p)
            return ring[:, u % RING, (p % 2) * PIECE:(p % 2 + 1) * PIECE]

        OV_TILES = CAP_TILES - 1
        OV_PE, OV_DVE = 6, 9 + 2 * T

        def overflow(eng, tile, skip, before=None, expert=None, tile_skip=None, after=None):
            eng.wait_ge(s_route, 1)
            any_over = eng.value_load(over[0:1, 0:1], min_val=0, max_val=SEQ)
            with eng.If(any_over > 0):
                if before:
                    before()
                count, per_expert = skip
                eng.sem_inc(count, 1)
                with eng.Fori(0, E) as e:
                    more = eng.value_load(over[0:1, bass.ds(e + E, 1)], min_val=0, max_val=SEQ)
                    with eng.If(more > 0):
                        if expert:
                            expert(e)
                        if tile:
                            with eng.Fori(0, OV_TILES) as j:
                                more_here = eng.value_load(over[0:1, bass.ds(e + (j + 1) * E, 1)], min_val=0, max_val=SEQ)
                                with eng.If(more_here > 0):
                                    tile(e, j, e * OV_TILES + j)
                                with eng.Else():
                                    before_tile, per_tile = tile_skip(e, j)
                                    eng.wait_ge(count, before_tile + 1)
                                    eng.sem_inc(count, per_tile)
                    with eng.Else():
                        eng.wait_ge(count, e * per_expert + 1)
                        eng.sem_inc(count, per_expert)
                if after:
                    after()

        block = ctx.enter_context(nc.Block())

        @block.sync
        def _(sp):
            def freed(u):
                q = ada_third(u)
                if q is not None:
                    sp.wait_ge(ada_used, 8 * q + u - ada_units[q] + 1)
                elif u < FIRST_MOE_UNIT:
                    first = next(n for n in range(7) if chunk_units[n] <= u < chunk_units[n] + 2)
                    sp.wait_ge(lo_pool, 4 * first + 2 * (u - chunk_units[first]) + 2)
                else:
                    n = 2 * (u - FIRST_MOE_UNIT) + 2
                    sp.wait_ge(lo_pool, FIRST_MOE_PIECE + pool_count(n))
                    sp.wait_ge(lo_dve, dve_count(n))

            def load(u, src, k):
                sp.dma_start(slot_view(u, k), src).then_inc(landed[u % RING], 16)

            def slot_view(u, k):
                return ring[:, u % RING, :].rearrange("p (k n) -> p k n", k=k)

            def vec(row, n, src):
                sp.dma_start(vrows[row:row + n, :], src).then_inc(vec_in, 16)

            vec(C_COL, K, c.rearrange("b (k p) -> (b k) p", p=P))
            vec(N1_COL, K, norm1_g.rearrange("b (k p) -> (b k) p", p=P))
            vec(N2_COL, K, norm2_g.rearrange("b (k p) -> (b k) p", p=P))
            vec(MIX_COL, K, mix_out_g.rearrange("b (k p) -> (b k) p", p=P))
            vec(CW_COL, 3 * CT, conv_w.rearrange("b w (k p) -> (b w k) p", p=P))
            vec(CB_COL, CT, conv_b.rearrange("b (k p) -> (b k) p", p=P))
            vec(SPB_COL, H, sp_b[0])
            vec(ADA_COL, 2 * K, b_ada[:, 0:UNIT].rearrange("b (k p) -> (b k) p", p=P))
            for u in range(FIRST_MOE_UNIT):
                if u >= RING:
                    freed(u - RING)
                q = ada_third(u)
                if q is not None:
                    k = u - ada_units[q]
                    sp.dma_start(ring[:, u % RING, :], w_ada[0, k * P:(k + 1) * P, q * UNIT:(q + 1) * UNIT])\
                        .then_inc(landed[u % RING], 16)
                else:
                    n = next(n for n in range(7) if chunk_units[n] <= u < chunk_units[n] + 2)
                    half = u - chunk_units[n]
                    if n < 5:
                        j = CHUNK_COLS[n]
                        load(u, w_in_v[:, 4 * half:4 * half + 4, j * BANK:(j + 1) * BANK], 4)
                    else:
                        half = W_OUT_HALF[half]
                        load(u, w_out_v[:, 4 * half:4 * half + 4, (n - 5) * BANK:(n - 4) * BANK], 4)

            def expert_unit(u, n, e):
                if n < 4:
                    w = exp_w_gate if n < 2 else exp_w_up
                    load(u, rows_of(w, e)[:, 4 * (n % 2):4 * (n % 2) + 4, :], 4)
                else:
                    load(u, rows_of(exp_w_down, e - 1)[:, 2 * (n - 4):2 * (n - 4) + 2, :], 2)

            for u in range(FIRST_MOE_UNIT, FIRST_MOE_UNIT + 16):
                freed(u - RING)
                s, n = (0, u - 38) if u < 42 else ((u - 36) // 6, u % 6)
                expert_unit(u, n, s)

            def keep_y(e, parity, count):
                sp.wait_ge(s_yev, count)
                sp.dma_start(y_rows_dram[e, 0:P, :], y_rows[:, parity, :]).then_inc(y_stored[parity], 16)

            def load_step(i, h, store=True):
                for n in range(STEP_UNITS):
                    sp.wait_ge(piece_used, i * (2 * STEP_PIECES) + (moe_piece(h, 2 * n + 1) + 1))
                    expert_unit(54 + 6 * h + n, n, i * 2 + (3 + h))
                    if n == 3 and store:
                        keep_y(i * 2 + (h - 1), (h + 1) % 2, i * 4 + 2 * h)

            load_step(0, 0, store=False)
            load_step(0, 1)
            with sp.Fori(1, 6) as i:
                load_step(i, 0)
                load_step(i, 1)
            load_step(6, 0)
            for n in range(2):
                sp.wait_ge(lo_pool, POOL_0 + 13 * POOL_STEP + pool_count(2 * n + 2))
                sp.wait_ge(lo_dve, DVE_0 + 13 * DVE_STEP + dve_count(2 * n + 2))
                load(132 + n, rows_of(exp_w_down, E - 1)[:, 2 * n:2 * n + 2, :], 2)
            for e in range(12, E - 1):
                keep_y(e, e % 2, 2 * e + 2)
            sp.wait_ge(piece_used, moe_piece(E - 1, 3) + 1)
            sp.dma_start(fin_b[:], final_g.rearrange("(a d) -> a d", a=1).broadcast_to([P, D])).then_inc(fin_in, 16)

            def ov_tokens():
                sp.dma_start(ov_h2[:], h2_dram.rearrange("(t p) d -> p t d", p=P)).then_inc(ov_h2_in, 16)

            def ov_weights(e):
                sp.wait_ge(ov_pe, e * (OV_TILES * OV_PE) + 1)
                for n, w in enumerate((exp_w_gate, exp_w_up, exp_w_down)):
                    src = w[0, bass.ds(e, 1)].rearrange("a (k p) n -> p (a k) n", p=P)
                    sp.dma_start(ov_w[:, n, :].rearrange("p (k n) -> p k n", n=w.shape[3]), src).then_inc(ov_in, 16)

            overflow(sp, None, (ov_in, 48), ov_tokens, ov_weights)
            for t in range(T - 1):
                sp.wait_ge(s_t4, t + 1)
                sp.dma_start(out[0, t * P:(t + 1) * P, :], out_sb[:, t, :]).then_inc(out_st, 16)
            for half in range(2):
                cols = slice(half * BANK, (half + 1) * BANK)
                sp.wait_ge(s_t4, T + half)
                sp.dma_start(out[0, SEQ - P:SEQ, cols], out_sb[:, T - 1, cols]).then_inc(out_st, 16)
            sp.wait_ge(out_st, 16 * (T + 1))

        @block.gpsimd
        def _(pool):
            nc.gpsimd.memset(ident[:], 0.0).then_inc(pool_step, 1)
            pool.wait_ge(pool_step, 1)
            nc.gpsimd.affine_select(out=ident[:], in_=ident[:], compare_op=ALU.not_equal, fill=1.0,
                                    base=0, pattern=[[-1, P]], channel_multiplier=1).then_inc(consts, 1)
            nc.gpsimd.memset(ada0[:], 0.0).then_inc(s_zeroed, 1)

            def low(p, ready):
                pool.wait_ge(hi_ready, ready)
                nc.gpsimd.tensor_tensor(w_lo[:, p % SLOTS, :], raw_of(p), w_hi[:, p % SLOTS, :].bitcast(F32),
                                        ALU.subtract).then_inc(lo_pool, 1)

            def gather(e, parity, count, before=None):
                nc.gpsimd.tensor_copy(tok_now[:, parity:parity + 1], tok_of[:, bass.ds(e, 1)]).then_inc(pool_step, 1)
                pool.wait_ge(pool_step, count + 2)
                if before:
                    before()
                pool.indirect_dma_start(x_rows[:, parity, :], None, h2_dram,
                                        bass.IndirectOffsetOnAxis(ap=tok_now[:, parity:parity + 1], axis=0))\
                    .then_inc(gathered[parity], 16)

            for p in range(FIRST_MOE_PIECE):
                if p == 14:
                    pool.wait_ge(s_mixed, 4)
                    nc.gpsimd.memset(ada1[:], 0.0).then_inc(s_zeroed, 1)
                    nc.gpsimd.memset(ada2[:], 0.0).then_inc(s_zeroed, 1)
                low(p, p + 1)
            pool.wait_ge(s_x1, 2 * T)
            nc.gpsimd.iota(slot_iota[:], pattern=[[1, P]], base=0, channel_multiplier=0,
                           allow_small_or_imprecise_dtypes=True).then_inc(s_late, 1)
            nc.gpsimd.iota(tok_id[:], pattern=[[P, T]], base=0, channel_multiplier=1,
                           allow_small_or_imprecise_dtypes=True).then_inc(s_late, 1)
            nc.gpsimd.memset(ones16[:], 1.0).then_inc(s_late, 1)
            pool.wait_ge(s_late, 3)
            nc.gpsimd.affine_select(out=low_tri[:], in_=ones16[:], compare_op=ALU.is_gt, fill=0.0,
                                    base=0, pattern=[[1, P]], channel_multiplier=-1).then_inc(s_late, 1)
            for t in range(T):
                pool.wait_ge(s_h2a, t + 1)
                nc.gpsimd.tensor_tensor(h2_tok[:, t % 2, :], h2_tok[:, t % 2, :], shift2_b[:], ALU.add).then_inc(s_h2b, 1)
                pool.wait_ge(s_h2b, t + 1)
                pool.dma_start(h2_dram[t * P:(t + 1) * P, :], h2_tok[:, t % 2, :]).then_inc(s_h2st[t % 2], 16)
            low(FIRST_MOE_PIECE + 2, FIRST_MOE_PIECE + 3)
            for b in range(2):
                pool.wait_ge(s_h2st[b], 32)
            pool.wait_ge(s_tok, 1)
            for e in range(2):
                gather(e, e, e)
            low(FIRST_MOE_PIECE + 5, FIRST_MOE_PIECE + 6)
            pool.wait_ge(s_xrTh, 2)
            gather(2, 0, 2)

            def pool_step_of(i, h, fetch=True):
                def low_of(n):
                    low(moe_piece(h, n), i * (2 * STEP_PIECES) + (moe_piece(h, n) + 1))
                if fetch:
                    pool.wait_ge(s_xrTh, i * 4 + (2 * h + 4))
                    gather(i * 2 + (3 + h), (1 + h) % 2, i * 2 + (3 + h), lambda: low_of(2))
                else:
                    low_of(2)
                for n in range(3, STEP_PIECES):
                    if on_pool(n):
                        low_of(n)

            with pool.Fori(0, 6) as i:
                pool_step_of(i, 0)
                pool_step_of(i, 1)
            pool_step_of(6, 0)
            pool_step_of(6, 1, fetch=False)
            pool_step_of(7, 0, fetch=False)
            low(moe_piece(15, 2), moe_piece(15, 2) + 1)
            pool.wait_ge(s_route, 1)
            pool.wait_ge(piece_used, moe_piece(E - 3, 11) + 1)
            pool.wait_ge(y_stored[0], 16 * (E // 2))
            pool.wait_ge(y_stored[1], 16 * (E // 2 - 1))
            for t in range(T):
                for c in range(2):
                    pool.indirect_dma_start(y_back[:, t, c, :], None, y_dram,
                                            bass.IndirectOffsetOnAxis(ap=row_of[:, 4 * c + t:4 * c + t + 1], axis=0))\
                        .then_inc(s_back[t], 16)

        @block.scalar
        def _(act_e):

            def bias_rows(dst, q):
                for j in range(4):
                    col = q * UNIT + j * BANK
                    act_e.dma_start(dst[32 * j:32 * j + 1, :], b_ada[0:1, col:col + BANK]).then_inc(ada_b_in[q], 16)

            act_e.dma_start(w_s[:], sp_w[0].rearrange("h i j -> i h j")).then_inc(ws_in, 16)
            for t in range(T):
                act_e.dma_start(xs[:, t, :], x[0, t * P:(t + 1) * P, :]).then_inc(x_in[t], 16)
            act_e.dma_start(spg_b[:], sp_norm_g.broadcast_to([P, DS])).then_inc(spg_in, 16)
            act_e.wait_ge(s_vcols, 1)
            nc.scalar.activation(vcols[:, 0:K], vcols[:, 0:K], ACT.Silu).then_inc(s_silu_c, 1)
            act_e.wait_ge(s_eps, 1)
            for t in range(T):
                act_e.wait_ge(x_in[t], 16)
                nc.scalar.activation(square1[:], xs[:, t, :], ACT.Square, accum_out=ss1[:, t:t + 1]).then_inc(s_sq1, 1)
                act_e.wait_ge(s_sq1, t + 1)
            nc.scalar.activation(ss1, ss1, ACT.Sqrt, bias=epsc, scale=1.0 / D).then_inc(s_std1, 1)

            def high(p, u, i=0):
                if p % 2 == 0:
                    act_e.wait_ge(landed[u % RING], i * 16 + 16 * (u // RING + 1))
                if not (isinstance(i, int) and p < SLOTS):
                    act_e.wait_ge(piece_used, i * (2 * STEP_PIECES) + (p - SLOTS + 1))
                nc.scalar.activation(w_hi[:, p % SLOTS, :], raw_of(p), ACT.Copy).then_inc(hi_ready, 1)

            def high1(p):
                high(p, chunk_unit(p) if p < FIRST_MOE_PIECE else moe_unit(p))

            act_e.wait_ge(ada_used, 8)
            act_e.wait_ge(s_zeroed, 1)
            for j in (2, 3):
                r = slice(32 * j, 32 * j + 1)
                nc.scalar.activation(ada0[r, :], bank[r, 7, :], ACT.Copy).then_inc(s_ada_row, 1)
            act_e.wait_ge(s_mod1, 2)
            for k in range(K):
                act_e.wait_ge(s_xT, k + 1)
                nc.scalar.activation(bank[:, k, :], bank[:, k, :], ACT.Identity, bias=mod1[:, k:k + 1],
                                     scale=mod1[:, 8 + k:9 + k]).then_inc(s_modded, 1)
                if k % 2:
                    act_e.wait_ge(s_modded, k + 1)
                    nc.scalar.activation(hT_hi[:, k, :], bank[:, k, :], ACT.Copy).then_inc(s_hThi, 1)
                    high1(k // 2)
            for p in range(4, 8):
                high1(p)
            for t in range(T):
                wait_bank(act_e, 0, t)
                nc.scalar.activation(v_tok[:, t, :], bank[:, t, :], ACT.Gelu_apprx_tanh).then_inc(s_gelu, 1)
            for p in range(8, 12):
                high1(p)
            for t in range(T):
                wait_bank(act_e, 1, t)
                nc.scalar.activation(u_tok[:, t, :], bank[:, 4 + t, :], ACT.Gelu_apprx_tanh).then_inc(s_gelu, 1)
            act_e.wait_ge(s_vsq, 4)
            nc.scalar.activation(ssv, ssv, ACT.Sqrt, bias=epsc, scale=1.0 / DS).then_inc(s_vstd, 1)
            for p in range(12, 16):
                high1(p)
            for t in range(CT):
                wait_bank(act_e, 2, t)
                nc.scalar.activation(z[:, t, :], bank[:, t, :], ACT.Copy).then_inc(s_c, 1)
            act_e.wait_ge(s_mixed, 4)
            act_e.wait_ge(s_zeroed, 3)
            bias_rows(ada1, 1)
            bias_rows(ada2, 2)
            for j in range(2):
                act_e.dma_start(n2_row[32 * j:32 * j + 1, :], norm2_g[0:1, j * BANK:(j + 1) * BANK]).then_inc(n2_in, 16)
            act_e.wait_ge(s_gated, H)
            for t in range(T):
                nc.scalar.activation(bank[:, 4 + t, :], u_tok[:, t, :], ACT.Square).then_inc(s_spsq, 1)
            act_e.wait_ge(s_spred, T)
            nc.scalar.activation(ssp, ssp, ACT.Sqrt, bias=epsc, scale=1.0 / HD).then_inc(s_spstd, 1)
            for p in range(16, 20):
                high1(p)
            for t in range(CT):
                act_e.wait_ge(s_y, t + 1)
                nc.scalar.activation(y_sq[:, t, :], y_conv[:, t, :], ACT.Square).then_inc(s_ysq, 1)
            for m in range(4):
                act_e.wait_ge(s_spT, m + 1)
                nc.scalar.activation(hT_hi[:, 4 + m, :], bank[:, m, :], ACT.Copy,
                                     scale=vcols[:, MIX_COL + 4 + m:MIX_COL + 5 + m]).then_inc(s_sphi, 1)
            for p in range(20, 22):
                high1(p)
            act_e.wait_ge(s_nsum, 1)
            nc.scalar.activation(conv_std[:], bank[:, 6, :], ACT.Sqrt, bias=epsc, scale=1.0 / HD).then_inc(s_nstd, 1)
            for p in range(22, 24):
                high1(p)
            act_e.wait_ge(s_adaq, 10)
            for n, src in enumerate((ada1, ada2)):
                act_e.dma_start(rows_dram[n], src[0:P:32, :]).then_inc(s_rows_out, 16)
            for p in range(24, 26):
                high1(p)
            act_e.wait_ge(s_rows_out, 32)
            act_e.dma_start(g1_b[:], row_of_dram(0, 0)).then_inc(s_g1_in, 16)
            act_e.dma_start(g2_b[:], row_of_dram(1, 2)).then_inc(s_rows_in, 16)
            act_e.wait_ge(s_yT, 8)
            act_e.dma_start(scale2_b[:], row_of_dram(1, 0)).then_inc(s_rows_in, 16)
            act_e.dma_start(shift2_b[:], row_of_dram(0, 2)).then_inc(s_rows_in, 16)
            high1(26)
            high1(27)
            act_e.wait_ge(s_fold, 2)
            act_e.dma_start(rw[:, :, 0:E], router_w.rearrange("(k p) e -> p k e", p=P)).then_inc(rw_in, 16)
            for t in range(T):
                act_e.wait_ge(s_x1, T + t + 1)
                nc.scalar.activation(h2_tok[:, t % 2, :], xs[:, t, :], ACT.Square,
                                     accum_out=ss2[:, t:t + 1]).then_inc(s_sq2, 1)
                act_e.wait_ge(s_sq2, t + 1)
                nc.scalar.activation(ss2[:, t:t + 1], ss2[:, t:t + 1], ACT.Sqrt, bias=epsc,
                                     scale=1.0 / D).then_inc(s_std2, 1)
            act_e.dma_start(rb_b[:], router_b.rearrange("(a e) -> a e", a=1).broadcast_to([P, E])).then_inc(rb_in, 16)
            for n, k in enumerate(K2_ORDER[:5]):
                act_e.wait_ge(s_x2T, n + 1)
                nc.scalar.activation(h2T[:, k, :], bank[:, k, :], ACT.Identity, bias=mod2[:, k:k + 1],
                                     scale=mod2[:, 8 + k:9 + k]).then_inc(s_h2T, 1)
            for p in range(28, 31):
                high1(p)
            act_e.wait_ge(s_lg, 1)
            nc.scalar.activation(rt(0), bank[:, 1, 0:T * E], ACT.Exp, scale=-1.0).then_inc(s_exp2, 1)
            high1(31)

            def turned_high(count):
                for half in range(2):
                    act_e.wait_ge(s_xrTh, count + half)
                    nc.scalar.activation(xT_hi[:, 4 * half:4 * half + 4, :], bank_k(4 + half), ACT.Copy).then_inc(s_xThi, 1)

            def act_high(count):
                act_e.wait_ge(s_fT, count)
                nc.scalar.activation(fT_hi[:], bank_k(4), ACT.Copy).then_inc(s_fThi, 1)

            def silu(parity, count):
                act_e.wait_ge(piece_used, count)
                nc.scalar.activation(act[:, parity, :], bank[:, 2 * parity, :], ACT.Silu).then_inc(s_silu, 1)

            turned_high(1)
            for p in range(32, 36):
                high1(p)
            silu(0, FIRST_MOE_PIECE + 4)
            for n in range(2):
                high1(moe_piece(0, n))
            turned_high(3)
            for n in range(2, 4):
                high1(moe_piece(0, n))

            def act_step_of(i, h, turn=True):
                def high_of(n):
                    p = moe_piece(h, n)
                    high(p, moe_unit(p), i)
                for n in range(4, 8):
                    high_of(n)
                act_high(i * 2 + (h + 1))
                silu((1 + h) % 2, i * (2 * STEP_PIECES) + (moe_piece(h, 0) + 4))
                for n in range(8, 12):
                    high_of(n)
                if turn:
                    turned_high(i * 4 + (2 * h + 5))
                for n in range(12, 16):
                    high_of(n)

            with act_e.Fori(0, 7) as i:
                act_step_of(i, 0)
                act_step_of(i, 1)
            act_step_of(7, 0, turn=False)
            act_e.wait_ge(s_pickT, 1)
            nc.scalar.activation(last_spread[:], bank_k(0), ACT.Copy).then_inc(s_spread, 1)
            act_high(E)

            def ov_act_tile(e, j, tile):
                act_e.wait_ge(ov_pe, tile * OV_PE + 3)
                nc.scalar.activation(ov_act[:], bank[:, 2, :], ACT.Silu).then_inc(ov_silu, 1)

            overflow(act_e, ov_act_tile, (ov_silu, OV_TILES), tile_skip=lambda e, j: (e * OV_TILES + j, 1))
            nc.scalar.activation(rsp[:, 0:1], epsc, ACT.Sqrt)
            for t in range(T):
                act_e.wait_ge(s_t2, t + 1)
                nc.scalar.activation(out_sb[:, t, :], xs[:, t, :], ACT.Square, accum_out=ss1[:, t:t + 1]).then_inc(s_sq3, 1)
                act_e.wait_ge(s_sq3, t + 1)
                nc.scalar.activation(ss1[:, t:t + 1], ss1[:, t:t + 1], ACT.Sqrt, bias=epsc, scale=1.0 / D).then_inc(s_t3, 1)

        @block.vector
        def _(dve):
            v = nc.vector
            chain = [0]

            def link(ins):
                chain[0] += 1
                ins.then_inc(step, 1)
                dve.wait_ge(step, chain[0])

            v.memset(epsc, EPS).then_inc(s_eps, 1)
            link(v.memset(head_ones4[:], 0.0))
            for j in range(4):
                v.memset(head_ones4[0:64, 32 * j:32 * j + 1], 1.0).then_inc(s_ho, 1)
                v.memset(head_ones4[64:P, 32 * j + 1:32 * j + 2], 1.0).then_inc(s_ho, 1)
            dve.wait_ge(s_ho, 8)
            v.tensor_copy(head_ones[:], head_ones4[:, 0:32]).then_inc(s_hones, 1)
            dve.wait_ge(s_vT, 1)
            v.tensor_copy(vcols[:], bank[:, 6, 0:NV]).then_inc(s_vcols, 1)
            dve.wait_ge(s_vcols, 1)
            v.tensor_scalar(vcols[:, ADA_COL + K:NV], vcols[:, ADA_COL + K:NV], 1.0, None, ALU.add).then_inc(s_vcols, 1)
            dve.wait_ge(s_expT, 1)
            v.tensor_copy(expand[:], bank[:, 3, 0:P]).then_inc(s_expand, 1)
            dve.wait_ge(ws_in, 16)
            v.memset(w_s[0:64, :, 64:P], 0.0).then_inc(s_ws_masked, 1)
            for a in range(2):
                dve.wait_ge(s_wsT, a + 1)
                v.tensor_copy(wsT[:, 4 * a:4 * a + 4, :], bank_k(4 + a)).then_inc(s_wsT_sb, 1)
            dve.wait_ge(s_std1, 1)
            link(v.reciprocal(r1, ss1))
            dve.wait_ge(consts, 1)
            for t in range(T):
                v.tensor_scalar(diag1[:, t, :], ident[:], r1[:, t:t + 1], None, ALU.mult).then_inc(s_diag1, 1)
            dve.wait_ge(ada_used, 8)
            dve.wait_ge(s_zeroed, 1)
            for j in range(2):
                r = slice(32 * j, 32 * j + 1)
                v.tensor_copy(ada0[r, :], bank[r, 7, :]).then_inc(s_ada_row, 1)
            dve.wait_ge(s_vcols, 2)
            dve.wait_ge(s_cols, 1)
            v.tensor_tensor(mod1[:].rearrange("p (r j) -> p r j", r=4), turned_rows(4),
                            vcols[:, ADA_COL:NV].rearrange("p (r j) -> p r j", r=4), ALU.add).then_inc(s_mod1, 1)
            dve.wait_ge(s_mod1, 1)
            v.tensor_tensor(mod1[:, 8:16], mod1[:, 8:16], vcols[:, N1_COL:N1_COL + 8], ALU.mult).then_inc(s_mod1, 1)
            for k in range(K):
                if k % 2:
                    dve.wait_ge(s_hThi, k // 2 + 1)
                else:
                    dve.wait_ge(s_modded, k + 1)
                    link(v.tensor_copy(hT_hi[:, k, :], bank[:, k, :]))
                v.tensor_tensor(hT_lo[:, k, :], bank[:, k, :], hT_hi[:, k, :].bitcast(F32), ALU.subtract).then_inc(s_hT, 1)
            for t in range(T):
                dve.wait_ge(s_gelu, t + 1)
                v.tensor_tensor_reduce(bank[:, t, :], v_tok[:, t, :], v_tok[:, t, :], 1.0, 0.0, ALU.mult, ALU.add,
                                       ssv[:, t:t + 1]).then_inc(s_vsq, 1)
            dve.wait_ge(s_vstd, 1)
            link(v.reciprocal(rv, ssv))
            dve.wait_ge(spg_in, 16)
            for t in range(T):
                v.scalar_tensor_tensor(out=v_tok[:, t, :], in0=v_tok[:, t, :], scalar=rv[:, t:t + 1], in1=spg_b[:],
                                       op0=ALU.mult, op1=ALU.mult).then_inc(s_vn, 1)
            dve.wait_ge(s_gelu, 2 * T)
            for h in range(H):
                dve.wait_ge(s_mixed, h // 2 + 1)
                u_h = u_tok[:, :, h * HD:(h + 1) * HD]
                s_h = bank[:, 4 + h // 2, (h % 2) * 256:(h % 2 + 1) * 256].rearrange("p (t d) -> p t d", t=T)
                v.scalar_tensor_tensor(out=u_h, in0=s_h, scalar=vcols[:, SPB_COL + h:SPB_COL + h + 1], in1=u_h,
                                       op0=ALU.add, op1=ALU.mult).then_inc(s_gated, 1)
            for t in range(T):
                dve.wait_ge(s_spsq, t + 1)
                v.tensor_reduce(ssp[:, t * H:(t + 1) * H], bank[:, 4 + t, :].rearrange("p (h d) -> p h d", h=H),
                                AX.X, ALU.add).then_inc(s_spred, 1)
            dve.wait_ge(s_spstd, 1)
            link(v.reciprocal(rsp, ssp))
            for t in range(T):
                y_h = u_tok[:, t, :].rearrange("p (h d) -> p h d", h=H)
                v.tensor_tensor(y_h, y_h, rsp[:, t * H:(t + 1) * H].rearrange("p (h o) -> p h o", o=1).broadcast_to([P, H, HD]),
                                ALU.mult).then_inc(s_spn, 1)
            dve.wait_ge(ada_b_in[1], 64)
            dve.wait_ge(ada_used, 16)
            for j in range(4):
                r = slice(32 * j, 32 * j + 1)
                v.tensor_tensor(ada1[r, :], ada1[r, :], bank[r, 7, :], ALU.add).then_inc(s_adaq, 1)
            for t in range(CT):
                dve.wait_ge(s_c, t + 1)
                wait_bank(dve, 3, t)
                v.tensor_tensor(z[:, t, :], z[:, t, :], bank[:, t, :], ALU.mult).then_inc(s_z, 1)
                dve.wait_ge(s_z, t + 1)
                link(v.tensor_scalar(y_conv[:, t, :], z[:, t, :], vcols[:, CW_COL + 8 + t:CW_COL + 9 + t],
                                     vcols[:, CB_COL + t:CB_COL + t + 1], ALU.mult, ALU.add))
                for lag in (1, 2):
                    cw = CW_COL + 4 * (2 - lag) + t
                    link(v.scalar_tensor_tensor(out=y_conv[:, t, lag:], in0=z[:, t, :SEQ - lag], scalar=vcols[:, cw:cw + 1],
                                                in1=y_conv[:, t, lag:], op0=ALU.mult, op1=ALU.add))
            for t in range(CT):
                wait_bank(dve, 4, t)
                v.tensor_tensor(y_conv[:, t, :], y_conv[:, t, :], bank[:, 4 + t, :], ALU.mult).then_inc(s_y, 1)
            for m in range(4):
                dve.wait_ge(s_sphi, m + 1)
                v.scalar_tensor_tensor(out=hT_lo[:, 4 + m, :], in0=bank[:, m, :],
                                       scalar=vcols[:, MIX_COL + 4 + m:MIX_COL + 5 + m],
                                       in1=hT_hi[:, 4 + m, :].bitcast(F32), op0=ALU.mult, op1=ALU.subtract).then_inc(s_yT, 1)
            dve.wait_ge(s_nstd, 1)
            v.reciprocal(conv_r[:], conv_std[:]).then_inc(s_rc, 1)
            dve.wait_ge(ada_b_in[2], 64)
            dve.wait_ge(n2_in, 32)
            dve.wait_ge(ada_used, 24)
            for j in range(4):
                r = slice(32 * j, 32 * j + 1)
                v.tensor_tensor(ada2[r, :], ada2[r, :], bank[r, 5, :], ALU.add).then_inc(s_adaq, 1)
            dve.wait_ge(s_adaq, 8)
            for j in range(2):
                r = slice(32 * j, 32 * j + 1)
                v.scalar_tensor_tensor(out=ada2[r, :], in0=ada2[r, :], scalar=1.0, in1=n2_row[r, :],
                                       op0=ALU.add, op1=ALU.mult).then_inc(s_adaq, 1)
            for t in range(CT):
                dve.wait_ge(s_exp, t + 1)
                link(v.scalar_tensor_tensor(out=y_conv[:, t, :], in0=y_conv[:, t, :],
                                            scalar=vcols[:, MIX_COL + t:MIX_COL + t + 1], in1=bank[:, t, :],
                                            op0=ALU.mult, op1=ALU.mult))
                link(v.tensor_copy(hT_hi[:, t, :], y_conv[:, t, :]))
                v.tensor_tensor(hT_lo[:, t, :], y_conv[:, t, :], hT_hi[:, t, :].bitcast(F32), ALU.subtract).then_inc(s_yT, 1)
            dve.wait_ge(s_cols2, 2)
            v.tensor_copy(mod2[:, 0:8].rearrange("p (r j) -> p r j", r=2), turned_rows(0)[:, 2:4, :]).then_inc(s_mod2, 1)
            v.tensor_copy(mod2[:, 8:16].rearrange("p (r j) -> p r j", r=2), turned_rows(1)[:, 0:2, :]).then_inc(s_mod2, 1)
            v.memset(rw[:], 0.0).then_inc(s_fold, 1)
            dve.wait_ge(consts, 1)
            v.tensor_reduce(fold[:], ident[:].rearrange("p (j e) -> p e j", j=4), AX.X, ALU.add).then_inc(s_fold, 1)
            def add_projection(half, t):
                cols = slice(half * BANK, (half + 1) * BANK)
                b = t + 4 * (1 - half)
                wait_bank(dve, 5 + half, t)
                link(v.tensor_tensor(bank[:, b, :], bank[:, b, :], g1_b[:, cols], ALU.mult))
                v.tensor_tensor(xs[:, t, cols], xs[:, t, cols], bank[:, b, :], ALU.add).then_inc(s_x1, 1)

            def scale_identity(t):
                dve.wait_ge(s_std2, t + 1)
                link(v.reciprocal(r2[:, t:t + 1], ss2[:, t:t + 1]))
                v.tensor_scalar(diag2[:, t, :], ident[:], r2[:, t:t + 1], None, ALU.mult).then_inc(s_diag2, 1)

            def scale_tokens(t):
                if t >= 2:
                    dve.wait_ge(s_h2st[t % 2], 16)
                v.scalar_tensor_tensor(out=h2_tok[:, t % 2, :], in0=xs[:, t, :], scalar=r2[:, t:t + 1], in1=scale2_b[:],
                                       op0=ALU.mult, op1=ALU.mult).then_inc(s_h2a, 1)

            dve.wait_ge(s_g1_in, 16)
            for t in range(T):
                add_projection(0, t)
            dve.wait_ge(s_cols2, 2)
            dve.wait_ge(s_rows_in, 48)
            for t in range(T):
                add_projection(1, t)
                if t >= 2:
                    scale_identity(t - 2)
            for t in (2, 3):
                scale_identity(t)
            for t in range(2):
                scale_tokens(t)
            for n in range(3):
                k = K2_ORDER[5 + n]
                dve.wait_ge(s_x2T, 5 + n + 1)
                v.tensor_scalar(h2T[:, k, :], bank[:, k, :], mod2[:, 8 + k:9 + k], mod2[:, k:k + 1],
                                ALU.mult, ALU.add).then_inc(s_h2T_dve, 1)
            dve.wait_ge(s_late, 4)
            eidx, gidx = numbers[:], numbers[:, :, 0:G]
            link(v.tensor_scalar(eidx, slot_iota[:, 0:E].rearrange("p (o e) -> p o e", o=1).broadcast_to([P, T, E]), 1.0, None, ALU.mult))
            dve.wait_ge(s_lgT, 1)
            v.tensor_copy(lgT[:], bank[:, 4, :]).then_inc(s_lgTs, 1)
            scale_tokens(2)

            def r4(n, m=E):
                return routing[:, n, 0:T * m].rearrange("p (t e) -> p t e", t=T)

            scores, sel, S1, S2, oh1, oh2 = r4(1), r4(2), r4(3), r4(4), r4(5), r4(6)
            rowbase = r4(22)
            scale_tokens(3)
            dve.wait_ge(s_exp2, 1)
            link(v.tensor_scalar(rt(8), rt(0), 1.0, None, ALU.add))
            link(v.reciprocal(rt(1), rt(8)))
            dve.wait_ge(rb_in, 16)
            link(v.tensor_tensor(sel, scores, rb_b[:].rearrange("p (o e) -> p o e", o=1).broadcast_to([P, T, E]), ALU.add))
            pair = rt(2).rearrange("p (g a b) -> p g a b", a=2, b=2)

            def half_of(n):
                return routing[:, n, 0:2 * T * G].rearrange("p (g a) -> p g a", a=2)

            link(v.tensor_tensor(half_of(9), pair[:, :, :, 0], pair[:, :, :, 1], ALU.max))
            link(v.tensor_tensor(half_of(10), pair[:, :, :, 0], pair[:, :, :, 1], ALU.min))

            def g1(n):
                return routing[:, n, 0:T * G]

            link(v.tensor_tensor(g1(11), half_of(9)[:, :, 0], half_of(9)[:, :, 1], ALU.max))
            link(v.tensor_tensor(g1(12), half_of(9)[:, :, 0], half_of(9)[:, :, 1], ALU.min))
            link(v.tensor_tensor(g1(13), half_of(10)[:, :, 0], half_of(10)[:, :, 1], ALU.max))
            link(v.tensor_tensor(g1(12), g1(12), g1(13), ALU.max))
            link(v.tensor_tensor(g1(11), g1(11), g1(12), ALU.add))

            def first_highest(values, idx, width, tmp, one):
                m = routing[:, tmp, 0:T]
                mb = m.rearrange("p (t o) -> p t o", o=1).broadcast_to([P, T, width])
                cand = r4(tmp + 1, width)
                link(v.tensor_reduce(m, values, AX.X, ALU.max))
                link(v.tensor_tensor(cand, values, mb, ALU.is_equal))
                link(v.scalar_tensor_tensor(out=cand, in0=cand, scalar=-2.0 * E, in1=idx, op0=ALU.mult, op1=ALU.add))
                link(v.tensor_reduce(m, cand, AX.X, ALU.min))
                link(v.tensor_tensor(one, cand, mb, ALU.is_equal))

            in_group = r4(14, G)
            first_highest(r4(11, G), gidx, G, 15, in_group)
            link(v.tensor_scalar(r4(17, G), in_group, BIG, -BIG, ALU.mult, ALU.add))
            gp = routing[:, 17, 0:T * G].rearrange("p (g o) -> p g o", o=1).broadcast_to([P, T * G, 4])
            link(v.tensor_tensor(rt(3).rearrange("p (g o) -> p g o", o=4), rt(2).rearrange("p (g o) -> p g o", o=4), gp, ALU.add))
            first_highest(S1, eidx, E, 15, oh1)
            link(v.scalar_tensor_tensor(out=S2, in0=oh1, scalar=-3 * BIG, in1=S1, op0=ALU.mult, op1=ALU.add))
            first_highest(S2, eidx, E, 15, oh2)
            v.tensor_tensor(mask16[:].rearrange("p (t e) -> p t e", t=T), oh1, oh2, ALU.add).then_inc(s_mask, 1)
            for n, one in enumerate((oh1, oh2)):
                v.tensor_tensor(tok_val[:, n, :].rearrange("p (t e) -> p t e", t=T), one,
                                tok_id[:].rearrange("p (t o) -> p t o", o=1).broadcast_to([P, T, E]), ALU.mult).then_inc(s_tokval, 1)
            dve.wait_ge(s_rank, 1)
            for n, one in enumerate((oh1, oh2)):
                if n == 0:
                    placed = routing[:, 15:17, :].rearrange("p c (t e) -> p (c t) e", e=E)
                    for m in range(2):
                        v.tensor_tensor(r4(15 + m), (oh1, oh2)[m], bank[:, 2, 0:T * E].rearrange("p (t e) -> p t e", t=T),
                                        ALU.mult).then_inc(s_counts, 1)
                    dve.wait_ge(s_counts, 2)
                    link(v.tensor_reduce(place_f, placed, AX.X, ALU.add))
                for t in range(T):
                    v.tensor_scalar(onehot[:, n, t, :], slot_iota[:], place_f[:, n * T + t:n * T + t + 1], None,
                                    ALU.is_equal).then_inc(s_oh, 1)
            v.tensor_copy(over_f[0:1, E:2 * E], bank[0:1, 2, T * E:T * E + E]).then_inc(s_counts, 1)
            dve.wait_ge(s_idx, 1)
            v.tensor_copy(tok_of[:], bank[:, 3, 0:E]).then_inc(s_tok, 1)
            link(v.scalar_tensor_tensor(out=rt(15), in0=bank[:, 2, 0:T * E], scalar=1.0, in1=mask16[:], op0=ALU.add, op1=ALU.mult))
            link(v.tensor_scalar(rankm[:], rt(15), -1.0, None, ALU.add))

            def low(p, ready):
                dve.wait_ge(hi_ready, ready)
                v.tensor_tensor(w_lo[:, p % SLOTS, :], raw_of(p), w_hi[:, p % SLOTS, :].bitcast(F32),
                                ALU.subtract).then_inc(lo_dve, 1)

            def low_static(ns):
                for n in ns:
                    if not on_pool(n):
                        low(FIRST_MOE_PIECE + n, FIRST_MOE_PIECE + n + 1)

            low_static(range(0, 4))

            def turned_low(count):
                for half in range(2):
                    dve.wait_ge(s_xThi, count + half)
                    v.tensor_tensor(xT_lo[:, 4 * half:4 * half + 4, :], bank_k(4 + half),
                                    xT_hi[:, 4 * half:4 * half + 4, :].bitcast(F32), ALU.subtract).then_inc(s_xTlo, 1)

            def act_low(count):
                dve.wait_ge(s_fThi, count)
                v.tensor_tensor(fT_lo[:], bank_k(4), fT_hi[:].bitcast(F32), ALU.subtract).then_inc(s_fTlo, 1)

            def gated_act(parity, count, used):
                dve.wait_ge(s_silu, count)
                dve.wait_ge(piece_used, used)
                v.tensor_tensor(act[:, parity, :], act[:, parity, :], bank[:, 2 * parity + 1, :], ALU.mult).then_inc(s_act, 1)

            def keep_outputs(parity, used, stored=None):
                if stored is not None:
                    dve.wait_ge(y_stored[parity], stored)
                dve.wait_ge(piece_used, used)
                for half in range(2):
                    cols = slice(half * BANK, (half + 1) * BANK)
                    v.tensor_tensor(y_rows[:, parity, cols], bank[:, 6 + half, :], g2_b[:, cols], ALU.mult).then_inc(s_yev, 1)

            turned_low(1)
            low_static(range(4, 8))
            for n in range(2):
                low(moe_piece(0, n), moe_piece(0, n) + 1)
            turned_low(3)
            gated_act(0, 1, FIRST_MOE_PIECE + 8)
            low(moe_piece(0, 3), moe_piece(0, 3) + 1)

            def dve_step_of(i, h, turn=True, keep=True, stored=True, extra=(None, None, None)):
                def more(n):
                    if extra[n]:
                        extra[n]()
                def low_of(n):
                    m = n % STEP_PIECES
                    if not on_pool(m):
                        low(moe_piece(h, n), i * (2 * STEP_PIECES) + (moe_piece(h, n) + 1))
                if keep:
                    keep_outputs((1 + h) % 2, i * (2 * STEP_PIECES) + moe_piece(h, 0), (i * 16 + (16 * h - 16)) if stored else None)
                for n in range(4, 8):
                    low_of(n)
                act_low(i * 2 + (h + 1))
                more(0)
                for n in range(8, 11):
                    low_of(n)
                more(1)
                gated_act((1 + h) % 2, i * 2 + (h + 2), i * (2 * STEP_PIECES) + (moe_piece(h, 0) + 8))
                low_of(11)
                more(2)
                if turn:
                    turned_low(i * 4 + (2 * h + 5))
                for n in range(12, 15):
                    low_of(n)
                if not turn:
                    keep_outputs(0, moe_piece(15, 0), 16 * 7)
                low_of(15)

            def weights_of_choice(n):
                link(v.tensor_tensor(r4(15), (oh1, oh2)[n], scores, ALU.mult))
                link(v.tensor_reduce(routing[:, 18, n * T:(n + 1) * T], r4(15), AX.X, ALU.add))

            def normalise():
                link(v.tensor_tensor(routing[:, 19, 0:T], routing[:, 18, 0:T], routing[:, 18, T:2 * T], ALU.add))
                link(v.reciprocal(routing[:, 19, T:2 * T], routing[:, 19, 0:T]))
                for n in range(2):
                    link(v.tensor_tensor(w_tok[:, n * T:(n + 1) * T], routing[:, 18, n * T:(n + 1) * T],
                                         routing[:, 19, T:2 * T], ALU.mult))

            def weights_of_experts():
                for n, one in enumerate((oh1, oh2)):
                    link(v.tensor_tensor(r4(15 + n), one, w_tok[:, n * T:(n + 1) * T].rearrange("p (t o) -> p t o", o=1)
                                         .broadcast_to([P, T, E]), ALU.mult))
                link(v.tensor_tensor(comb[:], rt(15), rt(16), ALU.add))

            def rows_of_places():
                link(v.tensor_scalar(rowbase, eidx, float(P), None, ALU.mult))
                link(v.tensor_scalar(rt(17), rankm[:], float(P), None, ALU.is_lt))
                link(v.scalar_tensor_tensor(out=r4(17), in0=eidx, scalar=float(E - 1), in1=r4(17), op0=ALU.is_lt, op1=ALU.mult))
                link(v.tensor_tensor(rt(15), rankm[:], rt(22), ALU.add))
                link(v.tensor_tensor(rt(15), rt(15), rt(17), ALU.mult))

            def rows_of_choice(n):
                one = (oh1, oh2)[n]
                link(v.tensor_tensor(r4(16), one, r4(15), ALU.mult))
                link(v.tensor_reduce(row_f[:, n * T:(n + 1) * T], r4(16), AX.X, ALU.add))
                link(v.tensor_tensor(r4(16), one, r4(17), ALU.mult))
                link(v.tensor_reduce(routing[:, 18, n * T:(n + 1) * T], r4(16), AX.X, ALU.add))
                link(v.tensor_tensor(w_tok[:, n * T:(n + 1) * T], w_tok[:, n * T:(n + 1) * T],
                                     routing[:, 18, n * T:(n + 1) * T], ALU.mult))

            def overflows_of_any():
                link(v.tensor_copy(row_of[:], row_f))
                dve.wait_ge(s_counts, 3)
                link(v.tensor_reduce(over_f[0:1, 0:1], over_f[0:1, 16:32], AX.X, ALU.max))
                link(v.tensor_scalar(over_f[0:1, 0:1], over_f[0:1, 0:1], -float(P), 0.0, ALU.add, ALU.max))
                link(v.memset(over_f[0:1, 1:16], 0.0))

            def overflows_of_experts():
                for j in (2, 3, 1):
                    link(v.tensor_scalar(over_f[0:1, E * j:E * j + E], over_f[0:1, E:2 * E], -float(P * j), 0.0, ALU.add, ALU.max))
                v.tensor_copy(over[0:1, :], over_f[0:1, 0:64]).then_inc(s_route, 1)

            def last_picks():
                for t in range(T):
                    col = t * E + E - 1
                    v.tensor_scalar(last_pick[:, t, :], slot_iota[:], rankm[:, col:col + 1], comb[:, col:col + 1],
                                    ALU.is_equal, ALU.mult).then_inc(s_pick, 1)

            dve_step_of(0, 0, keep=False, extra=(lambda: weights_of_choice(0), lambda: weights_of_choice(1), normalise))
            dve_step_of(0, 1, stored=False, extra=(weights_of_experts, rows_of_places, lambda: rows_of_choice(0)))
            dve_step_of(1, 0, stored=False, extra=(lambda: rows_of_choice(1), overflows_of_any, overflows_of_experts))
            last_picks()
            dve_step_of(1, 1)
            with dve.Fori(2, 7) as i:
                dve_step_of(i, 0)
                dve_step_of(i, 1)
            dve_step_of(7, 0, turn=False)
            act_low(E)
            dve.wait_ge(s_pickT, 1)
            for t in range(T):
                v.tensor_scalar(diag_w[:, t, :], ident[:], w_tok[:, t:t + 1], None, ALU.mult).then_inc(s_diag_w, 1)
            keep_outputs(1, moe_piece(15, 4), 16 * 7)

            def ov_expert(e):
                dve.wait_ge(ov_h2_in, 16)
                dve.wait_ge(ov_dve, e * (OV_TILES * OV_DVE + 2) + 1)
                v.tensor_copy(ov_rank[:], rankm[:].rearrange("p (t e) -> p t e", e=E)[:, :, bass.ds(e, 1)]
                              .rearrange("p t o -> p (t o)")).then_inc(ov_dve, 1)
                v.tensor_copy(ov_comb[:], comb[:].rearrange("p (t e) -> p t e", e=E)[:, :, bass.ds(e, 1)]
                              .rearrange("p t o -> p (t o)")).then_inc(ov_dve, 1)

            def ov_dve_tile(e, j, tile):
                base = tile * OV_DVE + e * 2 + 3
                pe_base = tile * OV_PE + 1
                dve.wait_ge(ov_dve, base)
                v.tensor_scalar(ov_rank[:], ov_rank[:], -float(P), None, ALU.add).then_inc(ov_dve, 1)
                dve.wait_ge(ov_dve, base + 1)
                for t in range(T):
                    v.tensor_scalar(ov_pick[:, t, :], slot_iota[:], ov_rank[:, t:t + 1], None, ALU.is_equal).then_inc(ov_dve, 1)
                dve.wait_ge(ov_pe, pe_base + 1)
                for half in range(2):
                    v.tensor_copy(ov_x[:, 4 * half:4 * half + 4, :], bank_k(half)).then_inc(ov_dve, 1)
                for t in range(T):
                    v.tensor_scalar(ov_pick[:, t, :], ov_pick[:, t, :], ov_comb[:, t:t + 1], None, ALU.mult).then_inc(ov_dve, 1)
                dve.wait_ge(ov_pe, pe_base + 2)
                dve.wait_ge(ov_silu, tile + 2)
                v.tensor_tensor(ov_act[:], ov_act[:], bank[:, 3, :], ALU.mult).then_inc(ov_dve, 1)
                dve.wait_ge(ov_pe, pe_base + 3)
                v.tensor_copy(ov_f[:], bank_k(4)).then_inc(ov_dve, 1)
                dve.wait_ge(ov_pe, pe_base + 4)
                v.tensor_copy(ov_spread[:], bank_k(5)).then_inc(ov_dve, 1)
                dve.wait_ge(ov_pe, pe_base + 5)
                for half in range(2):
                    cols = slice(half * BANK, (half + 1) * BANK)
                    v.tensor_tensor(ov_y[:, cols], bank[:, 6 + half, :], g2_b[:, cols], ALU.mult).then_inc(ov_dve, 1)
                dve.wait_ge(ov_pe, pe_base + 6)
                v.tensor_tensor(xs[:].rearrange("p t (h n) -> p (t h) n", h=2), xs[:].rearrange("p t (h n) -> p (t h) n", h=2),
                                bank[:], ALU.add).then_inc(ov_dve, 1)

            overflow(dve, ov_dve_tile, (ov_dve, OV_TILES * OV_DVE + 2), None, ov_expert,
                     lambda e, j: ((e * OV_TILES + j) * OV_DVE + e * 2 + 2, OV_DVE))

            def finish(t):
                dve.wait_ge(s_t3, t + 1)
                nc.vector.reciprocal(r1[:, t:t + 1], ss1[:, t:t + 1]).then_inc(s_r3, 1)
                dve.wait_ge(s_r3, t + 1)
                if t == 0:
                    dve.wait_ge(fin_in, 16)
                for cols in (slice(0, D),) if t < T - 1 else (slice(0, BANK), slice(BANK, D)):
                    v.scalar_tensor_tensor(out=out_sb[:, t, cols], in0=xs[:, t, cols], scalar=r1[:, t:t + 1],
                                           in1=fin_b[:, cols], op0=ALU.mult, op1=ALU.mult).then_inc(s_t4, 1)

            def add_back(t):
                dve.wait_ge(s_back[t], 32)
                v.scalar_tensor_tensor(out=xs[:, t, :], in0=y_back[:, t, 1, :], scalar=w_tok[:, T + t:T + t + 1],
                                       in1=xs[:, t, :], op0=ALU.mult, op1=ALU.add).then_inc(s_t1, 1)

            def add_spread(t):
                dve.wait_ge(s_t1, t + 1)
                dve.wait_ge(s_last, t + 1)
                v.tensor_tensor(xs[:, t, :].rearrange("p (h n) -> p h n", h=2), xs[:, t, :].rearrange("p (h n) -> p h n", h=2),
                                bank[:, 2 * t:2 * t + 2, :], ALU.add).then_inc(s_t2, 1)

            for t in range(T):
                add_back(t)
                add_spread(t)
                if t:
                    finish(t - 1)
            finish(T - 1)

        @block.tensor
        def _(pe):
            mm = nc.tensor.matmul
            pe.wait_ge(consts, 1)
            pe.wait_ge(vec_in, 16 * 8)
            nc.tensor.transpose(bank[:, 6, 0:NV], vrows[0:NV, :], ident[0:NV, 0:NV]).then_inc(s_vT, 1)
            pe.wait_ge(s_hones, 1)
            nc.tensor.transpose(bank[:, 3, 0:P], head_ones4[:], ident[:]).then_inc(s_expT, 1)

            def ada(q, b, between=None):
                for k in range(K):
                    u = ada_units[q] + k
                    pe.wait_ge(landed[u % RING], 16 * (u // RING + 1))
                    for j in range(4):
                        m = mm(bank[32 * j:32 * j + 1, b, :], vcols[:, k:k + 1], ring[:, u % RING, j * BANK:(j + 1) * BANK],
                               start=(k == 0), stop=(k == K - 1))
                    m.then_inc(ada_used, 1)
                    if between:
                        between(k)

            def turn_ada(src, b):
                for j in range(4):
                    m = nc.tensor.transpose(bank[:, b, j * P:(j + 1) * P], src[:, j * P:(j + 1) * P], ident[:])
                return m

            def turn_x(k, diag):
                for t in range(T):
                    m = mm(bank[:, k, t * P:(t + 1) * P], xs[:, t, k * P:(k + 1) * P], diag[:, t, :], start=True, stop=True)
                return m

            def in_ada0(k):
                if k == 2:
                    pe.wait_ge(s_ws_masked, 1)
                    for h in range(H):
                        m = nc.tensor.transpose(bank[:, 4 + h // 4, (h % 4) * P:(h % 4 + 1) * P], w_s[:, h, :], ident[:])
                        if h % 4 == 3:
                            m.then_inc(s_wsT, 1)
                if k in (5, 6):
                    pe.wait_ge(s_diag1, T)
                    pe.wait_ge(s_expand, 1)
                    for kk in range(2 * k - 10, 2 * k - 8):
                        turn_x(kk, diag1).then_inc(s_xT, 1)

            pe.wait_ge(s_silu_c, 1)
            ada(0, 7, in_ada0)
            pe.wait_ge(s_wsT_sb, 2)
            pe.wait_ge(s_ada_row, 4)
            turn_ada(ada0, 4).then_inc(s_cols, 1)
            for k in (5, 6, 7, 4):
                if k == 4:
                    pe.wait_ge(s_mod1, 2)
                m = turn_x(k, diag1)
            m.then_inc(s_xT, 4)

            def keep_clock_up(b, n):
                for _ in range(n):
                    mm(bank[:, b, :], ident[:], xs[:, 0, 0:BANK], start=True, stop=True)

            def three(out_ap, lhs, rhs, first, last):
                (a_hi, a_lo), (b_hi, b_lo) = lhs, rhs
                mm(out_ap, a_hi, b_hi, start=first, stop=False)
                mm(out_ap, a_lo, b_hi, start=False, stop=False)
                return mm(out_ap, a_hi, b_lo, start=False, stop=last)

            def weights(p, cols):
                v = [w[:, p % SLOTS, :].rearrange("p (k n) -> p k n", n=BANK) for w in (w_hi, w_lo)]
                return lambda kk: (v[0][:, kk, cols], v[1][:, kk, cols])

            def chunk(n, first_bank, by_token, k_order=range(8), between=None, before_last_bank=None):
                for q in range(4):
                    p = 4 * n + q
                    if n == 0:
                        pe.wait_ge(s_hT, max(2 * q + 2, 4))
                    pe.wait_ge(lo_pool, p + 1)
                    for b in range(4):
                        if q == 0 and b == 3 and before_last_bank:
                            before_last_bank()
                        tile = slice(b * P, (b + 1) * P)
                        for kk in range(2):
                            k = k_order[2 * q + kk]
                            first, last = (q == 0 and kk == 0), (q == 3 and kk == 1)
                            if by_token:
                                m = three(bank[:, first_bank + b, :], (hT_hi[:, k, tile], hT_lo[:, k, tile]),
                                          weights(p, slice(0, BANK))(kk), first, last)
                            else:
                                m = three(bank[:, first_bank + b, :], weights(p, tile)(kk),
                                          (hT_hi[:, k, :], hT_lo[:, k, :]), first, last)
                        if q == 3 and b < 3:
                            m.then_inc(s_chunk, 1)
                    m.then_inc(piece_used, 1)
                    if between:
                        between(q)

            pe.wait_ge(s_hT, 1)
            keep_clock_up(0, 3)
            chunk(0, 0, True)
            pe.wait_ge(s_hT, K)
            chunk(1, 4, True)
            pe.wait_ge(s_gelu, T)
            pe.wait_ge(s_vsq, T)
            chunk(2, 0, False)
            pe.wait_ge(s_gelu, 2 * T)
            pe.wait_ge(s_vn, T)
            for h in range(H):
                m = mm(bank[:, 4 + h // 2, (h % 2) * 256:(h % 2 + 1) * 256], wsT[:, h, :],
                       v_tok[:, :, h * HD:(h + 1) * HD], start=True, stop=True)
                if h % 2:
                    m.then_inc(s_mixed, 1)
            pe.wait_ge(s_c, CT)
            chunk(3, 0, False)
            pe.wait_ge(s_spred, T)
            ada(1, 7)
            chunk(4, 4, False, before_last_bank=lambda: pe.wait_ge(s_adaq, 4))
            pe.wait_ge(s_spn, T)
            pe.wait_ge(s_z, CT)
            for m_ in range(4):
                for t in range(T):
                    m = nc.tensor.transpose(bank[:, m_, t * P:(t + 1) * P], u_tok[:, t, m_ * P:(m_ + 1) * P], ident[:])
                m.then_inc(s_spT, 1)
            pe.wait_ge(s_ysq, CT)
            for t in range(CT):
                m = mm(bank[32 * t:32 * t + 32, 6, :], head_ones[:], y_sq[:, t, :], start=True, stop=True)
            m.then_inc(s_nsum, 1)
            pe.wait_ge(s_y, CT)
            ada(2, 5)
            pe.wait_ge(s_rc, 1)
            pe.wait_ge(s_yT, 4)
            for t in range(CT):
                mm(bank[:, t, :], expand[32 * t:32 * t + 32, :], conv_r[32 * t:32 * t + 32, :], start=True, stop=True).then_inc(s_exp, 1)

            def in_o0(q):
                if q == 1:
                    pe.wait_ge(s_yT, 8)
                    pe.wait_ge(s_adaq, 10)
                    turn_ada(ada1, 0).then_inc(s_cols2, 1)
                    turn_ada(ada2, 1).then_inc(s_cols2, 1)

            pe.wait_ge(s_adaq, 8)
            pe.wait_ge(s_nstd, 1)
            chunk(5, 4, True, [4, 5, 6, 7, 0, 1, 2, 3], in_o0)
            pe.wait_ge(s_mod2, 2)
            chunk(6, 0, True, [4, 5, 6, 7, 0, 1, 2, 3])

            def turn_tile(t, ks):
                for k in ks:
                    m = mm(bank[:, k, t * P:(t + 1) * P], xs[:, t, k * P:(k + 1) * P], diag2[:, t, :], start=True, stop=True)
                    if t == T - 1:
                        m.then_inc(s_x2T, 1)

            for t in range(T - 1):
                pe.wait_ge(s_diag2, t + 1)
                turn_tile(t, range(4, 8))
            pe.wait_ge(s_x1, 2 * T)
            for t in range(T - 1):
                turn_tile(t, range(0, 4))
            pe.wait_ge(s_diag2, T)
            turn_tile(T - 1, K2_ORDER)
            pe.wait_ge(rw_in, 16)
            for n, k in enumerate(K2_ORDER):
                if n < 5:
                    pe.wait_ge(s_h2T, n + 1)
                else:
                    pe.wait_ge(s_h2T_dve, n - 4)
                m = mm(bank[32 * (k % 4):32 * (k % 4) + 32, 4, :], rw[:, k, :], h2T[:, k, :], start=(n < 4), stop=(n >= 4))
            m.then_inc(s_lgT, 1)
            pe.wait_ge(s_lgTs, 1)
            for t in range(T):
                m = mm(bank[:, 1, t * E:(t + 1) * E], lgT[:, t * P:(t + 1) * P], fold[:, 0:E], start=True, stop=True)
            m.then_inc(s_lg, 1)
            pe.wait_ge(s_mask, 1)
            for t in range(T):
                for s in range(t + 1):
                    mm(bank[:, 2, t * E:(t + 1) * E], low_tri[:] if s == t else ones16[:], mask16[:, s * E:(s + 1) * E],
                       start=(s == 0), stop=(s == t))
            for s in range(T):
                m = mm(bank[:, 2, T * E:T * E + E], ones16[:], mask16[:, s * E:(s + 1) * E], start=(s == 0), stop=(s == T - 1))
            m.then_inc(s_rank, 1)
            pe.wait_ge(s_tokval, 2)
            for n in range(2 * T):
                pe.wait_ge(s_oh, n + 1)
                c, t = divmod(n, T)
                m = mm(bank[:, 3, 0:E], onehot[:, c, t, :], tok_val[:, c, t * E:(t + 1) * E], start=(n == 0), stop=(n == 2 * T - 1))
            m.then_inc(s_idx, 1)

            def turn_rows(parity, count):
                pe.wait_ge(gathered[parity], count)
                for k in range(K):
                    m = nc.tensor.transpose(bank[:, 4 + k // 4, (k % 4) * P:(k % 4 + 1) * P],
                                            x_rows[:, parity, k * P:(k + 1) * P], ident[:])
                    if k == 3:
                        m.then_inc(s_xrTh, 1)
                m.then_inc(s_xrTh, 1)

            def in_proj(h, i, ns, first_bank, tokens):
                for q, n in enumerate(ns):
                    if q % 2 == 0:
                        pe.wait_ge(s_xTlo, tokens - 1 + q // 2)
                    p = moe_piece(h, n) if h >= 0 else FIRST_MOE_PIECE + n
                    if h >= 0:
                        if on_pool(n):
                            pe.wait_ge(lo_pool, i * (2 * POOL_STEP) + (POOL_0 + POOL_STEP * h + pool_count(n + 1)))
                        else:
                            pe.wait_ge(lo_dve, i * (2 * DVE_STEP) + (DVE_0 + DVE_STEP * h + dve_count(n + 1)))
                    elif on_pool(n):
                        pe.wait_ge(lo_pool, FIRST_MOE_PIECE + pool_count(n + 1))
                    else:
                        pe.wait_ge(lo_dve, dve_count(n + 1))
                    for kk in range(2):
                        k = 2 * q + kk
                        m = three(bank[:, first_bank, :], (xT_hi[:, k, :], xT_lo[:, k, :]),
                                  weights(p, slice(0, BANK))(kk), k == 0, k == K - 1)
                    m.then_inc(piece_used, 1)

            def turn_act(parity, count):
                pe.wait_ge(s_act, count)
                for k in range(KF):
                    m = nc.tensor.transpose(bank[:, 4, k * P:(k + 1) * P], act[:, parity, k * P:(k + 1) * P], ident[:])
                m.then_inc(s_fT, 1)

            def out_proj(ps, waits):
                for k, p in enumerate(ps):
                    waits(k)
                    w = weights(p, slice(0, BANK))
                    for half in range(2):
                        m = three(bank[:, 6 + half, :], (fT_hi[:, k, :], fT_lo[:, k, :]), w(half), k == 0, k == KF - 1)
                    m.then_inc(piece_used, 1)

            keep_clock_up(6, 3)
            turn_rows(0, 16)
            in_proj(-1, 0, range(0, 4), 0, 2)
            in_proj(-1, 0, range(4, 8), 1, 2)
            turn_rows(1, 16)

            def pe_step_of(i, h, turn=True):
                par = (1 + h) % 2
                tokens = i * 4 + (2 * h + 4)
                in_proj(h, i, range(0, 4), 2 * par, tokens)
                turn_act(h % 2, i * 2 + (h + 1))
                in_proj(h, i, range(4, 8), 2 * par + 1, tokens)
                if turn:
                    pe.wait_ge(s_fTlo, i * 2 + (h + 1))
                    turn_rows(h % 2, i * 16 + 32)
                else:
                    pe.wait_ge(s_fTlo, i * 2 + (h + 1))
                if not (isinstance(i, int) and i == 0 and h == 0):
                    pe.wait_ge(s_yev, i * 4 + 2 * h)

                def waits(k):
                    n = 8 + k
                    if on_pool(n):
                        pe.wait_ge(lo_pool, i * (2 * POOL_STEP) + (POOL_0 + POOL_STEP * h + pool_count(n + 1)))
                    else:
                        pe.wait_ge(lo_dve, i * (2 * DVE_STEP) + (DVE_0 + DVE_STEP * h + dve_count(n + 1)))
                out_proj([moe_piece(h, 8 + k) for k in range(4)], waits)

            pe_step_of(0, 0)
            pe_step_of(0, 1)
            with pe.Fori(1, 7) as i:
                pe_step_of(i, 0)
                pe_step_of(i, 1)
            pe_step_of(7, 0, turn=False)
            pe.wait_ge(s_pick, T)
            for t in range(T):
                m = nc.tensor.transpose(bank[:, 0, t * P:(t + 1) * P], last_pick[:, t, :], ident[:])
            m.then_inc(s_pickT, 1)
            turn_act(1, E)
            keep_clock_up(1, 3)
            pe.wait_ge(s_fTlo, E)
            pe.wait_ge(s_yev, 2 * (E - 1))

            def last_waits(k):
                if on_pool(k):
                    pe.wait_ge(lo_pool, POOL_0 + POOL_STEP * 15 + pool_count(k + 1))
                else:
                    pe.wait_ge(lo_dve, DVE_0 + DVE_STEP * 15 + dve_count(k + 1))
            out_proj([moe_piece(15, k) for k in range(4)], last_waits)
            pe.wait_ge(s_spread, 1)

            def ov_pe_tile(e, j, tile):
                base = tile * OV_DVE + e * 2 + 3
                wg, wu = (ov_w[:, n, :].rearrange("p (k n) -> p k n", n=F) for n in range(2))
                wd = ov_w[:, 2, :].rearrange("p (k n) -> p k n", n=D)
                pe.wait_ge(ov_dve, base + 5)
                for k in range(K):
                    for t in range(T):
                        m = mm(bank[:, k // 4, (k % 4) * P:(k % 4 + 1) * P], ov_h2[:, t, k * P:(k + 1) * P],
                               ov_pick[:, t, :], start=(t == 0), stop=(t == T - 1))
                m.then_inc(ov_pe, 1)
                pe.wait_ge(ov_in, e * 48 + 49)
                pe.wait_ge(ov_dve, base + 7)
                for b, w in ((2, wg), (3, wu)):
                    for k in range(K):
                        m = mm(bank[:, b, :], ov_x[:, k, :], w[:, k, :], start=(k == 0), stop=(k == K - 1))
                m.then_inc(ov_pe, 1)
                pe.wait_ge(ov_dve, base + 12)
                for k in range(KF):
                    m = nc.tensor.transpose(bank[:, 4, k * P:(k + 1) * P], ov_act[:, k * P:(k + 1) * P], ident[:])
                m.then_inc(ov_pe, 1)
                for t in range(T):
                    m = nc.tensor.transpose(bank[:, 5, t * P:(t + 1) * P], ov_pick[:, t, :], ident[:])
                m.then_inc(ov_pe, 1)
                pe.wait_ge(ov_dve, base + 13)
                for half in range(2):
                    for k in range(KF):
                        m = mm(bank[:, 6 + half, :], ov_f[:, k, :], wd[:, k, half * BANK:(half + 1) * BANK],
                               start=(k == 0), stop=(k == KF - 1))
                m.then_inc(ov_pe, 1)
                pe.wait_ge(ov_dve, base + 16)
                for t in range(T):
                    for half in range(2):
                        m = mm(bank[:, 2 * t + half, :], ov_spread[:, t, :], ov_y[:, half * BANK:(half + 1) * BANK],
                               start=True, stop=True)
                m.then_inc(ov_pe, 1)

            def ov_read():
                pe.wait_ge(ov_dve, E * (OV_TILES * OV_DVE + 2) + 1)

            overflow(pe, ov_pe_tile, (ov_pe, OV_TILES * OV_PE),
                     tile_skip=lambda e, j: ((e * OV_TILES + j) * OV_PE, OV_PE), after=ov_read)
            pe.wait_ge(s_yev, 2 * E)
            pe.wait_ge(s_diag_w, T)
            for t in range(T):
                for half in range(2):
                    mm(bank[:, 2 * t + half, :], last_spread[:, t, :], y_rows[:, 1, half * BANK:(half + 1) * BANK],
                       start=True, stop=False)
                pe.wait_ge(s_back[t], 32)
                for half in range(2):
                    m = mm(bank[:, 2 * t + half, :], diag_w[:, t, :], y_back[:, t, 0, half * BANK:(half + 1) * BANK],
                           start=False, stop=True)
                m.then_inc(s_last, 1)


_INS = ['x', 'c', 'w_ada', 'b_ada', 'norm1_g', 'norm2_g', 'w_in', 'conv_w', 'conv_b', 'sp_norm_g', 'sp_w', 'sp_b',
        'mix_out_g', 'w_out', 'router_w', 'router_b', 'exp_w_gate', 'exp_w_up', 'exp_w_down', 'final_g']


def kernel(**inputs):
    import numpy as _np
    import concourse.bacc as _bacc
    from concourse.bass_utils import run_bass_kernel_spmd as _run

    nc = _bacc.Bacc("TRN2", target_bir_lowering=False, num_devices=1)
    arrays, args = {}, []
    for name in _INS:
        a = _np.ascontiguousarray(inputs[name])
        arrays[f"in_{name}"] = a
        args.append(nc.dram_tensor(f"in_{name}", a.shape, mybir.dt.from_np(a.dtype), kind="ExternalInput").ap())
    out = nc.dram_tensor("out", inputs["x"].shape, F32, kind="ExternalOutput").ap()
    trunk_kernel(nc, *args, out)
    r = _run(nc, [arrays], core_ids=[0])
    return r.results[0]["out"]
```
